# Optimizing a Trainium2 kernel written in Bass

```python
import math
import numpy as np
import jax
import jax.numpy as jnp
from jax import lax

D_MODEL = 1024
BATCH = 1
SEQ = 256
DEPTH = 1

N_META = 16
RMS_EPS = 1e-6
N_HEADS = 16
HEAD_DIM = 64
ATTN_WIDTH = N_HEADS * HEAD_DIM
ROT_DIM = HEAD_DIM // 4
ROPE_THETA = 500000.0
IDX_HEADS = 8
IDX_DIM = 64
IDX_ROT_DIM = IDX_DIM // 4
TOPK_KEYS_MAX = 256
Q_BLOCK = 128
SSM_INNER = 2 * D_MODEL
SSM_HEAD_DIM = 64
SSM_HEADS = SSM_INNER // SSM_HEAD_DIM
SSM_GROUPS = 4
SSM_STATE = 128
CONV_WIDTH = 4
CONV_CH = SSM_INNER + 2 * SSM_GROUPS * SSM_STATE
CHUNK = 128
N_EXPERTS = 32
TOP_K = 4
EXPERT_FF = D_MODEL
SWIGLU_LIMIT = 7.0
SWIGLU_ALPHA = 1.702
N_BRANCH = 2
IN_SPLITS = (ATTN_WIDTH, ATTN_WIDTH, ATTN_WIDTH, IDX_HEADS * IDX_DIM, IDX_DIM, IDX_HEADS, SSM_INNER, SSM_INNER, SSM_GROUPS * SSM_STATE, SSM_GROUPS * SSM_STATE, SSM_HEADS, N_BRANCH * D_MODEL)
IN_WIDTH = sum(IN_SPLITS)

kernel_name = "hybrid_dsa_ssd_moe_block"

def rms_norm(x, g):
    xf = x.astype(jnp.float32)
    y = xf * lax.rsqrt(jnp.mean(xf * xf, axis=-1, keepdims=True) + RMS_EPS)
    return (y * g.astype(jnp.float32)).astype(x.dtype)

def rope_partial(x, pos, rot_dim):
    half = rot_dim // 2
    inv_freq = jnp.exp(-math.log(ROPE_THETA) * jnp.arange(half, dtype=jnp.float32) / half)
    ang = pos.astype(jnp.float32)[:, None] * inv_freq[None, :]
    cos = jnp.cos(ang)[None, :, None, :]
    sin = jnp.sin(ang)[None, :, None, :]
    xr = x[..., :rot_dim].astype(jnp.float32)
    x1, x2 = xr[..., :half], xr[..., half:]
    rot = jnp.concatenate([x1 * cos - x2 * sin, x2 * cos + x1 * sin], axis=-1)
    return jnp.concatenate([rot.astype(x.dtype), x[..., rot_dim:]], axis=-1)

def sparse_rows(q, qi, wi, qpos, k_real, v_real, ki_real, k_meta, v_meta):
    n_keys = k_real.shape[0]
    k_sel = min(TOPK_KEYS_MAX, n_keys // 4)
    kpos = N_META + jnp.arange(n_keys)
    idx_logits = jnp.einsum('nhd,sd->nhs', qi, ki_real).astype(jnp.float32) * (IDX_DIM ** -0.5)
    score = jnp.einsum('nh,nhs->ns', wi.astype(jnp.float32), jax.nn.relu(idx_logits))
    score = jnp.where(kpos[None, :] <= qpos[:, None], score, -jnp.inf)
    _, sel = lax.top_k(score, k_sel)
    sel_ok = kpos[sel] <= qpos[:, None]
    k_g = k_real[sel]
    v_g = v_real[sel]
    scale = HEAD_DIM ** -0.5
    s_meta = jnp.einsum('nhd,mhd->nhm', q, k_meta).astype(jnp.float32) * scale
    s_sel = jnp.einsum('nhd,nkhd->nhk', q, k_g).astype(jnp.float32) * scale
    meta_ok = jnp.arange(N_META)[None, :] <= qpos[:, None]
    s = jnp.concatenate([jnp.where(meta_ok[:, None, :], s_meta, -jnp.inf),
                         jnp.where(sel_ok[:, None, :], s_sel, -jnp.inf)], axis=-1)
    p = jax.nn.softmax(s, axis=-1).astype(v_real.dtype)
    return (jnp.einsum('nhm,mhd->nhd', p[..., :N_META], v_meta)
            + jnp.einsum('nhk,nkhd->nhd', p[..., N_META:], v_g))

def indexer_sparse_attention(q, k, v, qi, ki, wi, pos):
    def one_seq(args):
        q_s, k_s, v_s, qi_s, ki_s, wi_s = args
        t = q_s.shape[0]

        def rows(blk):
            return sparse_rows(blk[0], blk[1], blk[2], blk[3],
                               k_s[N_META:], v_s[N_META:], ki_s[N_META:], k_s[:N_META], v_s[:N_META])

        out_meta = rows((q_s[:N_META], qi_s[:N_META], wi_s[:N_META], pos[:N_META]))
        n_blk = (t - N_META) // Q_BLOCK
        blks = tuple(a[N_META:].reshape((n_blk, Q_BLOCK) + a.shape[1:]) for a in (q_s, qi_s, wi_s, pos))
        out_real = lax.map(rows, blks).reshape((t - N_META,) + q_s.shape[1:])
        return jnp.concatenate([out_meta, out_real], axis=0)

    return lax.map(one_seq, (q, k, v, qi, ki, wi))

def segsum_exp(a_cs):
    l = a_cs.shape[-1]
    diff = a_cs[..., :, None] - a_cs[..., None, :]
    mask = jnp.tril(jnp.ones((l, l), dtype=bool))
    return jnp.exp(jnp.where(mask, diff, -jnp.inf))

def ssd_chunked(x, dt, a, bm, cm):
    b, length, h, p = x.shape
    g, n = bm.shape[2], bm.shape[3]
    e = h // g
    c = length // CHUNK
    xdt = (x * dt[..., None].astype(x.dtype)).reshape(b, c, CHUNK, g, e, p)
    adt = (dt * a).reshape(b, c, CHUNK, g, e).transpose(0, 3, 4, 1, 2)
    bc = bm.reshape(b, c, CHUNK, g, n)
    cc = cm.reshape(b, c, CHUNK, g, n)
    a_cs = jnp.cumsum(adt, axis=-1)
    lmat = segsum_exp(a_cs)
    cb = jnp.einsum('bclgn,bcsgn->bgcls', cc, bc)
    y_diag = jnp.einsum('bgcls,bgecls,bcsgep->bclgep', cb, lmat, xdt)
    decay_states = jnp.exp(a_cs[..., -1:] - a_cs)
    states = jnp.einsum('bcsgn,bgecs,bcsgep->bcgepn', bc, decay_states, xdt)
    chunk_decay = jnp.exp(a_cs[..., -1])

    def step(carry, inp):
        st, dec = inp
        return carry * dec[..., None, None] + st, carry

    init = jnp.zeros((b, g, e, p, n), dtype=states.dtype)
    _, prev = lax.scan(step, init, (jnp.moveaxis(states, 1, 0), jnp.moveaxis(chunk_decay, -1, 0)))
    y_off = jnp.einsum('bclgn,cbgepn,bgecl->bclgep', cc, prev, jnp.exp(a_cs))
    return (y_diag + y_off).reshape(b, length, h, p).astype(x.dtype)

def ssd_branch(z, xs, bm, cm, dt_raw, conv_w, conv_b, dt_bias, a_log, d_skip, ssm_norm_g):
    b, t, _ = xs.shape
    xbc = jnp.concatenate([xs, bm, cm], axis=-1)
    xbc = lax.conv_general_dilated(xbc, conv_w.astype(xbc.dtype)[:, None, :], (1,), [(CONV_WIDTH - 1, 0)],
                                   dimension_numbers=('NWC', 'WIO', 'NWC'), feature_group_count=CONV_CH)
    xbc = jax.nn.silu(xbc + conv_b)
    xs, bm, cm = jnp.split(xbc, [SSM_INNER, SSM_INNER + SSM_GROUPS * SSM_STATE], axis=-1)
    dt = jax.nn.softplus((dt_raw + dt_bias).astype(jnp.float32))
    a = -jnp.exp(a_log.astype(jnp.float32))
    pad = (-N_META) % CHUNK

    def padt(arr):
        return jnp.pad(arr, ((0, 0), (pad, 0)) + ((0, 0),) * (arr.ndim - 2))

    xh = xs.reshape(b, t, SSM_HEADS, SSM_HEAD_DIM)
    y = ssd_chunked(padt(xh), padt(dt), a,
                    padt(bm.reshape(b, t, SSM_GROUPS, SSM_STATE)),
                    padt(cm.reshape(b, t, SSM_GROUPS, SSM_STATE)))[:, pad:]
    y = y + xh * d_skip[:, None].astype(xh.dtype)
    y = y.reshape(b, t, SSM_INNER) * jax.nn.silu(z)
    yg = rms_norm(y.reshape(b, t, SSM_GROUPS, SSM_INNER // SSM_GROUPS), ssm_norm_g.reshape(SSM_GROUPS, -1))
    return yg.reshape(b, t, SSM_INNER)

def hybrid_mixer(hn, pos, w_in, conv_w, conv_b, dt_bias, a_log, d_skip, ssm_norm_g, w_o_attn, w_o_ssm, w_out):
    b, t, _ = hn.shape
    proj = hn @ w_in
    split_points = np.cumsum(IN_SPLITS)[:-1].tolist()
    q, k, v, qi, ki, wi, z, xs, bm, cm, dt_raw, gate_raw = jnp.split(proj, split_points, axis=-1)
    q = rope_partial(q.reshape(b, t, N_HEADS, HEAD_DIM), pos, ROT_DIM)
    k = rope_partial(k.reshape(b, t, N_HEADS, HEAD_DIM), pos, ROT_DIM)
    v = v.reshape(b, t, N_HEADS, HEAD_DIM)
    qi = rope_partial(qi.reshape(b, t, IDX_HEADS, IDX_DIM), pos, IDX_ROT_DIM)
    ki = rope_partial(ki.reshape(b, t, 1, IDX_DIM), pos, IDX_ROT_DIM)[:, :, 0]
    wi = wi * (IDX_HEADS ** -0.5)
    attn = indexer_sparse_attention(q, k, v, qi, ki, wi, pos).reshape(b, t, ATTN_WIDTH)
    ssm = ssd_branch(z, xs, bm, cm, dt_raw, conv_w, conv_b, dt_bias, a_log, d_skip, ssm_norm_g)
    gates = jax.nn.sigmoid(gate_raw.astype(jnp.float32)).astype(hn.dtype).reshape(b, t, N_BRANCH, D_MODEL)
    u = gates[:, :, 0] * (attn @ w_o_attn) + gates[:, :, 1] * (ssm @ w_o_ssm)
    return u @ w_out

def moe_ffn(hn, w_router, b_router, w_gate_up, b_gate_up, w_down, b_down):
    b, t, d = hn.shape
    tok = hn.reshape(b * t, d)
    logits = (tok @ w_router + b_router).astype(jnp.float32)
    top_v, top_i = lax.top_k(logits, TOP_K)
    top_w = jax.nn.softmax(top_v, axis=-1)
    dense_w = jnp.sum(jax.nn.one_hot(top_i, N_EXPERTS, dtype=jnp.float32) * top_w[..., None], axis=1).astype(tok.dtype)
    out = jnp.zeros_like(tok)
    for e in range(N_EXPERTS):
        gu = tok @ w_gate_up[e] + b_gate_up[e]
        gate, up = gu[:, :EXPERT_FF], gu[:, EXPERT_FF:]
        gate = jnp.minimum(gate, SWIGLU_LIMIT)
        up = jnp.clip(up, -SWIGLU_LIMIT, SWIGLU_LIMIT)
        act = (up + 1.0) * (gate * jax.nn.sigmoid(SWIGLU_ALPHA * gate))
        out = out + dense_w[:, e:e + 1] * (act @ w_down[e] + b_down[e])
    return out.reshape(b, t, d)

def setup_inputs(seed: int = 0) -> dict:
    key = jax.random.key(seed)
    ks = jax.random.split(key, 21)

    def nrm(k, shape, scale):
        return jax.random.normal(k, shape, jnp.float32) * scale

    dt0 = jnp.exp(jax.random.uniform(ks[6], (DEPTH, SSM_HEADS), jnp.float32) * (math.log(0.1) - math.log(0.001)) + math.log(0.001))
    return {
        'x': nrm(ks[0], (BATCH, SEQ, D_MODEL), 1.0),
        'meta_tokens': nrm(ks[1], (N_META, D_MODEL), 1.0),
        'norm1_g': 1.0 + nrm(ks[2], (DEPTH, D_MODEL), 0.05),
        'w_in': nrm(ks[3], (DEPTH, D_MODEL, IN_WIDTH), D_MODEL ** -0.5),
        'conv_w': nrm(ks[4], (DEPTH, CONV_WIDTH, CONV_CH), CONV_WIDTH ** -0.5),
        'conv_b': nrm(ks[5], (DEPTH, CONV_CH), 0.02),
        'dt_bias': dt0 + jnp.log(-jnp.expm1(-dt0)),
        'a_log': jnp.log(jax.random.uniform(ks[7], (DEPTH, SSM_HEADS), jnp.float32, 1.0, 16.0)),
        'd_skip': 1.0 + nrm(ks[8], (DEPTH, SSM_HEADS), 0.1),
        'ssm_norm_g': 1.0 + nrm(ks[9], (DEPTH, SSM_INNER), 0.05),
        'w_o_attn': nrm(ks[10], (DEPTH, ATTN_WIDTH, D_MODEL), ATTN_WIDTH ** -0.5),
        'w_o_ssm': nrm(ks[11], (DEPTH, SSM_INNER, D_MODEL), SSM_INNER ** -0.5),
        'w_out': nrm(ks[12], (DEPTH, D_MODEL, D_MODEL), D_MODEL ** -0.5),
        'norm2_g': 1.0 + nrm(ks[13], (DEPTH, D_MODEL), 0.05),
        'w_router': nrm(ks[14], (DEPTH, D_MODEL, N_EXPERTS), D_MODEL ** -0.5),
        'b_router': nrm(ks[15], (DEPTH, N_EXPERTS), 0.01),
        'w_gate_up': nrm(ks[16], (DEPTH, N_EXPERTS, D_MODEL, 2 * EXPERT_FF), D_MODEL ** -0.5),
        'b_gate_up': nrm(ks[17], (DEPTH, N_EXPERTS, 2 * EXPERT_FF), 0.02),
        'w_down': nrm(ks[18], (DEPTH, N_EXPERTS, EXPERT_FF, D_MODEL), EXPERT_FF ** -0.5),
        'b_down': nrm(ks[19], (DEPTH, N_EXPERTS, D_MODEL), 0.02),
        'final_g': 1.0 + nrm(ks[20], (D_MODEL,), 0.05),
    }

def reference(x, meta_tokens, norm1_g, w_in, conv_w, conv_b, dt_bias, a_log, d_skip, ssm_norm_g,
              w_o_attn, w_o_ssm, w_out, norm2_g, w_router, b_router, w_gate_up, b_gate_up,
              w_down, b_down, final_g):
    b = x.shape[0]
    meta = jnp.broadcast_to(meta_tokens.astype(x.dtype)[None], (b, N_META, D_MODEL))
    h = jnp.concatenate([meta, x], axis=1)
    pos = jnp.arange(h.shape[1], dtype=jnp.int32)
    for layer in range(DEPTH):
        hn = rms_norm(h, norm1_g[layer])
        h = h + hybrid_mixer(hn, pos, w_in[layer], conv_w[layer], conv_b[layer], dt_bias[layer],
                             a_log[layer], d_skip[layer], ssm_norm_g[layer], w_o_attn[layer],
                             w_o_ssm[layer], w_out[layer])
        h = h + moe_ffn(rms_norm(h, norm2_g[layer]), w_router[layer], b_router[layer],
                        w_gate_up[layer], b_gate_up[layer], w_down[layer], b_down[layer])
    h = rms_norm(h, final_g)
    return h[:, N_META:]


_drawn_inputs = setup_inputs


def setup_inputs(seed=0):
    import zlib

    import numpy as np

    out = dict(_drawn_inputs(seed))
    spreads = {}
    factors = {'b_gate_up': 5.693, 'b_down': 6.619}
    for name, (base, spread) in spreads.items():
        noise = np.random.default_rng([zlib.crc32(name.encode()), seed]).standard_normal(out[name].shape)
        drawn = base * np.exp(spread * noise) if base else spread * noise
        out[name] = jnp.asarray(drawn.astype(out[name].dtype))
    for name, factor in factors.items():
        out[name] = (out[name] * factor).astype(out[name].dtype)
    return out
```

```python
import math

import numpy as np

import concourse.bass as bass
from concourse import mybir

F32 = mybir.dt.float32
BF16 = mybir.dt.bfloat16
I32 = mybir.dt.int32
U32 = mybir.dt.uint32
ALU = mybir.AluOpType
ACT = mybir.ActivationFunctionType
AX = mybir.AxisListType

P = 128
D = 1024
SEQ = 256
N_META = 16
T_ALL = N_META + SEQ
RT = SEQ // P
KD = D // P
HEADS, HD = 16, 64
IDX_HEADS = 8
ROT = HD // 4
HALF = ROT // 2
ROPE_THETA = 500000.0
TOPK_KEYS = 64
SSM_INNER = 2 * D
SSM_HEADS = 32
GROUPS = 4
GH = SSM_HEADS // GROUPS
CONV_W = 4
CONV_TILES = (SSM_INNER + 2 * GROUPS * P) // P
EXPERTS = 32
TOP_K = 4
FF = D
LIMIT = 7.0
ALPHA = 1.702
EPS = 1e-6
SLOTS = 64
OVERFLOW_MAX = SEQ * TOP_K // SLOTS
MASKED = -3.0e38
PICKED = -3.3e38
UNROUTED = 1000.0

C_Q, C_K, C_V, C_QI = 0, 1024, 2048, 3072
C_KI, C_Z, C_X, C_DT, C_GATE = 3584, 3656, 5704, 8776, 8808

BLOCKS = (["S"] + [f"X{i}" for i in range(6)] + [f"Z{i}" for i in range(4)] + ["K0", "K1", "V0", "V1", "Q0", "Q1", "QI"]
          + [f"G{i}" for i in range(4)] + [f"OS{i}" for i in range(4)] + ["OA0", "OA1", "WO0", "WO1"])
NB = {name: n for n, name in enumerate(BLOCKS)}
RING = 5
SLOT = KD * 512


def constants():
    part = np.arange(P)[:, None]
    free = np.arange(P)[None, :]
    inv = np.exp(np.float32(-math.log(ROPE_THETA)) * np.arange(HALF, dtype=np.float32) / np.float32(HALF)).astype(np.float32)
    ang = np.arange(T_ALL, dtype=np.float32)[:, None] * inv[None, :]
    table = np.concatenate([np.cos(ang), np.sin(ang)], axis=1).astype(np.float32)
    rope = np.zeros((P, 3, ROT), np.float32)
    rope[:, 0] = table[N_META:N_META + P]
    rope[:, 1] = table[N_META + P:]
    rope[:N_META, 2] = table[:N_META]
    block = np.arange(1, 4)[:, None]
    parts = {
        "ident": (part == free),
        "tri_le": (part <= free),
        "tri_lt": (part < free),
        "ones": np.ones((P, P)),
        "slots": np.tile((SLOTS * np.arange(4)[:, None] + free % SLOTS).reshape(1, -1), (P, 1)),
        "causal": (free <= part),
        "causal_neg": np.where(free <= part, 0.0, MASKED),
        "experts": np.tile(np.arange(EXPERTS), (P, 1)),
        "row_expert": part % EXPERTS,
        "rope": rope.reshape(P, -1),
        "codes": np.tile((EXPERTS * block + np.arange(EXPERTS)[None, :]).reshape(1, -1), (P, 1)),
        "thresholds": np.tile((SLOTS * block + 0 * np.arange(EXPERTS)[None, :]).reshape(1, -1), (P, 1)),
        "turns": np.tile(np.arange(OVERFLOW_MAX), (P, 1)),
    }
    at, where = 0, {}
    for name, a in parts.items():
        where[name] = (at, at + a.shape[1])
        at += a.shape[1]
    return np.concatenate([a.astype(np.float32) for a in parts.values()], axis=1), where


def build(nc, x, meta_tokens, norm1_g, w_in, conv_w, conv_b, dt_bias, a_log, d_skip, ssm_norm_g,
          w_o_attn, w_o_ssm, w_out, norm2_g, w_router, b_router, w_gate_up, b_gate_up,
          w_down, b_down, final_g, out):
    table, where = constants()
    const_dram = nc.inline_tensor(table, name="const_table")

    def mem(name, cols, dt=F32):
        return nc.alloc_sbuf_tensor(name, [P, cols], dt)

    const = mem("const", table.shape[1])

    def cst(name):
        return const[:, where[name][0]:where[name][1]]

    ident, tri_le, tri_lt, ones = cst("ident"), cst("tri_le"), cst("tri_lt"), cst("ones")
    slots = cst("slots").rearrange("p (b s) -> p b s", b=4)
    rope_tab = cst("rope").rearrange("p (t c) -> p t c", t=3)
    weights = mem("weights", RING * SLOT)
    last_slot = mem("last_slot", SLOT)
    hrow = mem("hrow", RT * D)[:, :].rearrange("p (t d) -> p t d", t=RT)
    cols1 = mem("cols1", P)
    cols2 = mem("cols2", 24)
    small_t = mem("small", 3 * 104)
    small = small_t[:, :].rearrange("p (t c) -> p t c", t=3)
    stat = mem("stat", 64)
    hnT = mem("hnT", KD * T_ALL)[:, :].rearrange("p (k t) -> p k t", k=KD)
    ssmT = mem("ssmT", 16 * SEQ)[:, :].rearrange("p (k t) -> p k t", k=16)
    arena = mem("arena", 17600)
    conv_col = [[cols1[:, w * CONV_TILES + j:w * CONV_TILES + j + 1] for j in range(CONV_TILES)] for w in range(CONV_W)]
    convb_col = [cols1[:, 96 + j:97 + j] for j in range(CONV_TILES)]
    g1_col = [cols1[:, 120 + k:121 + k] for k in range(KD)]
    ssmg_cols = cols2[:, 0:16]
    g2_cols = cols2[:, 16:24]

    def carver(region, start=0):
        at = [start]

        def carve(n):
            at[0] += n
            assert at[0] <= region.shape[1], (at[0], region.shape)
            return region[:, at[0] - n:at[0]]
        return carve

    def split(ap, a):
        return ap.rearrange("p (a b) -> p a b", a=a)

    early = ssmT.rearrange("p k t -> p (k t)")
    xn = split(early[:, 0:3 * D], 3)
    rows1 = early[:, 3 * D:3 * D + P]
    rows2 = early[:, 3 * D + P:3 * D + 2 * P]
    carve = carver(arena)
    xbcT = split(carve(CONV_TILES * T_ALL), CONV_TILES)
    hmeta = carve(D)
    conv_acc = split(carve(3 * T_ALL), 3)
    bc = split(carve(3 * 32), 3)
    dt_x, dt_n, dt_e, dt_l, dtv, adt, wdec = (split(carve(96), 3) for _ in range(7))
    ea_log = carve(32)
    acs = split(carve(6 * 32), 6)
    eacs = split(carve(2 * 32), 2)
    cdec = carve(32)
    xr = split(carve(2 * 512), 2)
    xdt = split(carve(2 * 512), 2)
    xsk = split(carve(2 * 512), 2)
    br = split(carve(2 * P), 2)
    cbm = split(carve(2 * P), 2)
    ss_y = carve(16)
    argm = split(carve(2 * 512), 2)
    yrow = split(carve(2 * 512), 2)
    carve_last = carver(last_slot)
    xm = carve_last(512)
    xdec = carve_last(512)
    xmdec = carve_last(512)
    prev = split(carve_last(2 * 512), 2)
    gated = carve_last(512)
    tanh_z = carve_last(512)
    square_junk = carve_last(512)
    carve = carver(arena)
    kraw = split(carve(3 * D), 3)
    qiraw = split(carve(RT * 512), RT)
    gatesT = arena[:, 0:16 * SEQ].rearrange("p (k t) -> p k t", k=16)
    vraw = split(carve(3 * D), 3)
    qraw = split(carve(RT * D), RT)
    attnT = arena[:, 4096 + 3 * D:4096 + 5 * D].rearrange("p (k t) -> p k t", k=KD)
    qT = split(carve(KD * SEQ), KD)
    kT = split(carve(KD * T_ALL), KD)
    qiT = split(carve(4 * SEQ), 4)
    kidup = split(carve(RT * P), RT)
    kiT = carve(SEQ)
    amask = carve(2 * N_META + P + SEQ)
    carve_last = carver(last_slot)
    relu_b = split(carve_last(2 * 512), 2)
    score = split(carve_last(2 * SEQ), 2)
    work = split(carve_last(2 * SEQ), 2)
    ao = last_slot[:, 0:RT * D].rearrange("p (t d) -> p t d", t=RT)
    rope_tmp = split(carve_last(4 * 256), 4)
    sbuf_s = split(last_slot[:, 2048:2048 + 2 * 416], 2)
    top8 = carve(2 * 8 * 8)
    head_stat = split(carve(4 * 8), 4)
    pT_k = split(carve(2 * 384), 2)
    pT_m = split(last_slot[:, 2880:2880 + 512], 2)
    prob = split(carve(2 * 416), 2)
    carve = carver(arena)
    hn2 = split(carve(RT * D), RT)
    carve(2048)
    carve(3 * D)
    hn2T = split(carve(KD * SEQ), KD)
    w_r = split(carve(KD * EXPERTS), KD)
    br_bc = carve(EXPERTS)
    bdn = carve(D)
    gf_bc = carve(D)
    logit, dense_w, routed, posm = (split(carve(2 * EXPERTS), 2) for _ in range(4))
    v8, idxf, e4, w4 = (split(carve(16), 2) for _ in range(4))
    idx8 = split(mem("idx8", 16, U32)[:, :], 2)
    pick = split(carve(2 * 4 * EXPERTS), 2)
    dwT = split(carve(2 * P), 2)
    rstat = carve(16)
    count = carve(EXPERTS)
    flags, seq = carve(96), carve(96)
    n_over_f = carve(1)
    n_over = mem("n_over", 1, I32)
    codes_f = carve(OVERFLOW_MAX)
    codes = mem("codes", OVERFLOW_MAX, I32)
    xe_flat = hnT.rearrange("p k t -> p (k t)")[:, 0:512]
    xe = split(xe_flat, KD)
    actT = hnT.rearrange("p k t -> p (k t)")[:, 512:1024]
    y_sb = hnT.rearrange("p k t -> p (k t)")[:, 1024:1536]
    selT = hnT.rearrange("p k t -> p (k t)")[:, 1536:1792]
    late = ssmT.rearrange("p k t -> p (k t)")
    sel = split(late[:, 0:128], 2)
    selw = split(late[:, 128:384], 2)
    gmin, sig, upc, act = (late[:, 512 + 512 * i:1024 + 512 * i] for i in range(4))
    xrow = late[:, 2560:3072]
    one_hot = split(late[:, 2560:2560 + 96 * OVERFLOW_MAX], OVERFLOW_MAX)
    bias_raw = arena[0:EXPERTS, 2048:2048 + 2 * FF]
    bias_part16 = arena[0:EXPERTS, 4096:4096 + FF].bitcast(BF16)
    bias_parts = carve(FF).bitcast(BF16)
    one_expert = carve(SLOTS // 2).bitcast(BF16)
    final = split(arena[:, 4096:4096 + RT * D], RT)

    PS = nc.alloc_psum_tensor("ps", [P, 8, 512], F32)

    def bank(i):
        return PS[:, i, :]

    def wslot(name):
        n = NB[name] % RING
        return split(weights[:, n * SLOT:(n + 1) * SLOT], KD)

    gu_chunk = [split(weights[:, 0:4 * SLOT], KD)[:, k, :] for k in range(KD)]
    dn_chunk = [weights[:, 4 * SLOT + D * k:4 * SLOT + D * (k + 1)] for k in range(4)] \
        + [last_slot[:, D * k:D * (k + 1)] for k in range(4)]

    def sem(name):
        return nc.alloc_semaphore(name)

    const_in, rows_in, x_in, vec_in, late_in = sem("const_in"), sem("rows_in"), sem("x_in"), sem("vec_in"), sem("late_in")
    slot_in = [sem(f"slot_in{i}") for i in range(RING)]
    cols_ps, cols_ok = sem("cols_ps"), sem("cols_ok")
    sq1, rstd1, xn_ok, xnT_ps, hnT_ok = sem("sq1"), sem("rstd1"), sem("xn_ok"), sem("xnT_ps"), sem("hnT_ok")
    small_ps, small_ok = sem("small_ps"), sem("small_ok")
    zeroed = sem("zeroed")
    dt_dve, dt_act, acs_ps = sem("dt_dve"), sem("dt_act"), sem("acs_ps")
    conv_ps, conv_ok, xbc_ok = sem("conv_ps"), sem("conv_ok"), sem("xbc_ok")
    dve_chain, act_chain, pool_chain = sem("dve_chain"), sem("act_chain"), sem("pool_chain")
    xrow_ps, xrow_ok, bcb_ps, brow_ok, cbm_ok = sem("xrow_ps"), sem("xrow_ok"), sem("bcb_ps"), sem("brow_ok"), sem("cbm_ok")
    abc_ps, arg_ok, exp_ok, decay_ok = sem("abc_ps"), sem("arg_ok"), sem("exp_ok"), sem("decay_ok")
    pool_x = sem("pool_x")
    z_ps, tanh_ok, z_used = sem("z_ps"), sem("tanh_ok"), sem("z_used")
    state_ps, state_ok = sem("state_ps"), sem("state_ok")
    yd_ps, yo_ps, y_read = sem("yd_ps"), sem("yo_ps"), sem("y_read")
    y_ok, ysq_ok, yn_ok, yT_ps, ssmT_ok = sem("y_ok"), sem("ysq_ok"), sem("yn_ok"), sem("yT_ps"), sem("ssmT_ok")
    proj_ps, proj_ok = sem("proj_ps"), sem("proj_ok")
    kmeta_ps, kmeta_ok = sem("kmeta_ps"), sem("kmeta_ok")
    rope_ok = sem("rope_ok")
    turn_ps, turn_ok = sem("turn_ps"), sem("turn_ok")
    idx_ps, relu_ok, relu_used = sem("idx_ps"), sem("relu_ok"), sem("relu_used")
    mask_ok = sem("mask_ok")
    gate_ps, gate_ok, sigm_ok = sem("gate_ps"), sem("gate_ok"), sem("sigm_ok")
    s_ps, s_ok, prob_ok, pT_ps, pTk_ok, pTm_ok, pv_ps, ao_ok = (sem(n) for n in (
        "s_ps", "s_ok", "prob_ok", "pT_ps", "pTk_ok", "pTm_ok", "pv_ps", "ao_ok"))
    aoT_ps, attnT_ok = sem("aoT_ps"), sem("attnT_ok")
    os_ps, os_ok, oa_ps, uT_ok, wo_ps, h2_ok = (sem(n) for n in ("os_ps", "os_ok", "oa_ps", "uT_ok", "wo_ps", "h2_ok"))
    sq2, rstd2, hn2_ok, hn2T_ps, hn2T_ok = sem("sq2"), sem("rstd2"), sem("hn2_ok"), sem("hn2T_ps"), sem("hn2T_ok")
    logit_ps, negv_ok, e4_ok, dense_ok, route_ps, route_ok = (sem(n) for n in (
        "logit_ps", "negv_ok", "e4_ok", "dense_ok", "route_ps", "route_ok"))
    dwT_ok = sem("dwT_ok")
    bias_in, bias_part, gu_free, dn_free = sem("bias_in"), sem("bias_free"), sem("gu_free"), sem("dn_free")
    gu_in = [sem(f"gu_in{k}") for k in range(KD)]
    dn_in = [sem(f"dn_in{k}") for k in range(4)]
    hot_ok, bias_ps, xrow_ps2, xrow_sb, selw_ok = (sem(n) for n in ("hot_ok", "bias_ps", "xrow_ps2", "xrow_sb", "selw_ok"))
    sel_ok, selT_ps, selT_ok, xe_ps, xe_ok, gu_ps, gmin_ok, upc_ok, upg_ok, sig_ok, act_ok = (sem(n) for n in (
        "sel_ok", "selT_ps", "selT_ok", "xe_ps", "xe_ok", "gu_ps", "gmin_ok", "upc_ok", "upg_ok", "sig_ok", "act_ok"))
    actT_ps, actT_ok, y_ps, ysb_ok, scat_ps = sem("actT_ps"), sem("actT_ok"), sem("y_ps"), sem("ysb_ok"), sem("scat_ps")
    codes_ok, sum_ok, sq3, out_ok, out_in = sem("codes_ok"), sem("sum_ok"), sem("sq3"), sem("out_ok"), sem("out_in")

    def block_source(name):
        if name == "S":
            w = w_in[0].rearrange("(k p) n -> p k n", p=P)
            return [(w[:, :, C_KI:C_KI + 72], 0, 72), (w[:, :, C_DT:C_DT + 32], 72, 104)]
        if name[:2] == "OS":
            c, kk = int(name[2]) // 2, int(name[2]) % 2
            w = w_o_ssm[0].rearrange("(k p) n -> p k n", p=P)
            return [(w[:, KD * kk:KD * kk + KD, 512 * c:512 * c + 512], 0, 512)]
        if name[:2] in ("OA", "WO"):
            w = (w_o_attn if name[:2] == "OA" else w_out)[0].rearrange("(k p) n -> p k n", p=P)
            c = int(name[2])
            return [(w[:, :, 512 * c:512 * c + 512], 0, 512)]
        base = {"X": C_X, "Z": C_Z, "K": C_K, "V": C_V, "Q": C_Q, "G": C_GATE}[name[0]]
        at = C_QI if name == "QI" else base + 512 * int(name[1])
        return [(w_in[0].rearrange("(k p) n -> p k n", p=P)[:, :, at:at + 512], 0, 512)]

    def loaded(eng, name):
        n = NB[name]
        uses = sum(2 if BLOCKS[m] == "S" else 1 for m in range(n % RING, n + 1, RING))
        eng.wait_ge(slot_in[n % RING], 16 * uses)

    def used_up(name):
        i = int(name[-1]) if name[-1].isdigit() else 0
        return {"S": (small_ps, 1), "X": (conv_ps, 4 * i + 4), "Z": (z_ps, 2 * i + 2), "K": (kmeta_ps, 1), "V": (kmeta_ps, 1),
                "Q": (proj_ps, 14 if name == "QI" else 10 + 2 * i), "G": (gate_ps, 4 * i + 4), "OS": (os_ps, 4 * (i // 2) + 4),
                "OA": (oa_ps, 4 * i + 4), "WO": (wo_ps, 2 * i + 2)}[name if name == "S" else name[:-1]]

    def real(t):
        return slice(N_META + P * t, N_META + P * t + P)

    block = nc.Block()
    with block:
        @block.sync
        def _(sp):
            sp.dma_start(hrow, x[0].rearrange("(t p) d -> p t d", p=P)).then_inc(x_in, 16)
            sp.dma_start(hmeta[0:N_META, :], meta_tokens).then_inc(x_in, 16)
            for n, name in enumerate(BLOCKS):
                if n >= RING:
                    sp.wait_ge(*used_up(BLOCKS[n - RING]))
                for src, a, b in block_source(name):
                    sp.dma_start(wslot(name)[:, :, a:b], src).then_inc(slot_in[n % RING], 16)

            def load_expert(u, e, first=False):
                for k in range(KD):
                    if first:
                        sp.wait_ge(*used_up(("OS3", "OA0", "OA1", "WO0")[k // 2]))
                    else:
                        sp.wait_ge(gu_free, u * KD - KD + 1 + k)
                    sp.dma_start(gu_chunk[k], w_gate_up[0, bass.ds(e, 1), k * P:(k + 1) * P, :].rearrange("e p n -> (e p) n")).then_inc(gu_in[k], 16)
                for i in range(4):
                    if first:
                        sp.wait_ge(*used_up("WO1"))
                    else:
                        sp.wait_ge(dn_free, u * 4 - 3 + i)
                    src = w_down[0, bass.ds(e, 1), 2 * i * P:(2 * i + 2) * P, :].rearrange("e (k p) n -> p (e k) n", p=P)
                    region = weights[:, 4 * SLOT + 2 * D * i:4 * SLOT + 2 * D * (i + 1)] if i < 2 \
                        else last_slot[:, 2 * D * (i - 2):2 * D * (i - 1)]
                    sp.dma_start(split(region, 2), src).then_inc(dn_in[i], 16)

            sp.wait_ge(s_ps, HEADS)
            sp.dma_start(w_r, w_router[0].rearrange("(k p) n -> p k n", p=P)).then_inc(late_in, 16)
            sp.dma_start(br_bc, b_router[0].partition_broadcast(P)).then_inc(late_in, 16)
            sp.dma_start(bdn[0:EXPERTS, :], b_down[0]).then_inc(late_in, 16)
            sp.dma_start(gf_bc, final_g.partition_broadcast(P)).then_inc(late_in, 16)
            sp.wait_ge(uT_ok, KD)
            sp.dma_start(bias_raw, b_gate_up[0]).then_inc(bias_in, 16)
            load_expert(0, 0, first=True)
            with sp.Fori(1, EXPERTS) as u:
                load_expert(u, u)
            sp.wait_ge(route_ok, 1)
            over = sp.value_load(n_over[0:1, 0:1], min_val=0, max_val=OVERFLOW_MAX)
            with sp.If(over > 0):
                sp.wait_ge(codes_ok, 1)
                with sp.Fori(0, over) as j:
                    jj = nc.s_assert_within(j, 0, OVERFLOW_MAX - 1)
                    code = sp.value_load(codes[0:1, bass.ds(jj, 1)], min_val=0, max_val=4 * EXPERTS - 1)
                    load_expert(jj + EXPERTS, code % EXPERTS)
            for t in range(RT):
                sp.wait_ge(out_ok, t + 1)
                sp.dma_start(out[0, P * t:P * t + P, :], final[:, t, :]).then_inc(out_in, 16)
            sp.wait_ge(out_in, 16 * RT)

        @block.gpsimd
        def _(pool):
            def per_head(v):
                return v.unsqueeze(2).broadcast_to([v.shape[0], GH, HD])

            pool.wait_ge(vec_in, 48)
            pool.wait_ge(dt_dve, 5)
            for g in range(GROUPS):
                hs = slice(GH * g, GH * g + GH)
                for t in range(RT):
                    pool.wait_ge(xrow_ok, 3 * g + t + 1)
                    if g:
                        pool.wait_ge(yd_ps, 2 * g)
                        pool.wait_ge(y_ok, 2 * g)
                    pool.tensor_tensor(xdt[:, t].rearrange("p (h e) -> p h e", h=GH), xr[:, t].rearrange("p (h e) -> p h e", h=GH),
                                       per_head(dtv[:, t, hs]), ALU.mult).then_inc(pool_x, 1)
                    pool.tensor_tensor(xsk[:, t].rearrange("p (h e) -> p h e", h=GH), xr[:, t].rearrange("p (h e) -> p h e", h=GH),
                                       per_head(bc[:, 2, hs]), ALU.mult).then_inc(pool_x, 1)
                    if t == 0:
                        if g:
                            pool.wait_ge(state_ps, 2 * g)
                        pool.tensor_tensor(xdec.rearrange("p (h e) -> p h e", h=GH), xr[:, t].rearrange("p (h e) -> p h e", h=GH),
                                           per_head(wdec[:, 0, hs]), ALU.mult).then_inc(pool_x, 1)
                pool.wait_ge(xrow_ok, 3 * g + 3)
                pool.tensor_tensor(xmdec[0:N_META].rearrange("p (h e) -> p h e", h=GH), xm[0:N_META].rearrange("p (h e) -> p h e", h=GH),
                                   per_head(wdec[0:N_META, 2, hs]), ALU.mult).then_inc(pool_x, 1)
            pool.wait_ge(bias_in, 16)
            for i in range(3):
                pool.tensor_copy(bias_part16, bias_raw).then_inc(bias_part, 1)
                pool.wait_ge(bias_part, 2 * i + 1)
                pool.tensor_copy(bias_parts[EXPERTS * i:EXPERTS * i + EXPERTS, :], bias_part16)
                pool.tensor_tensor(bias_raw, bias_raw, bias_part16, ALU.subtract).then_inc(bias_part, 1)
                pool.wait_ge(bias_part, 2 * i + 2)

        @block.tensor
        def _(pe):
            def turn(dst, src):
                return pe.transpose(dst, src, ident[0:src.shape[0], 0:src.shape[0]])

            pe.wait_ge(const_in, 16)
            pe.wait_ge(rows_in, 80)
            turn(bank(0)[:, 0:P], rows1)
            turn(bank(0)[:, P:P + 24], rows2[0:24, :]).then_inc(cols_ps, 1)
            pe.wait_ge(xn_ok, 3)
            pe.wait_ge(cols_ok, 1)
            for k in range(KD):
                turn(bank(k)[:, 0:N_META], xn[0:N_META, 2, P * k:P * k + P])
                turn(bank(k)[:, real(0)], xn[:, 0, P * k:P * k + P])
                turn(bank(k)[:, real(1)], xn[:, 1, P * k:P * k + P]).then_inc(xnT_ps, 1)

            pe.wait_ge(hnT_ok, KD)
            loaded(pe, "S")
            for t in range(3):
                rows = real(t) if t < 2 else slice(0, N_META)
                m = P if t < 2 else N_META
                for k in range(KD):
                    mm = pe.matmul(bank(0)[0:m, 104 * t:104 * t + 104], hnT[:, k, rows], wslot("S")[:, k, 0:104],
                                   start=(k == 0), stop=(k == KD - 1))
            mm.then_inc(small_ps, 1)

            for j in range(CONV_TILES):
                name = f"X{j // 4}"
                if j % 4 == 0:
                    loaded(pe, name)
                if j >= 7:
                    pe.wait_ge(conv_ok, j - 6)
                for k in range(KD):
                    mm = pe.matmul(bank(1 + j % 7)[:, 0:T_ALL], wslot(name)[:, k, P * (j % 4):P * (j % 4) + P], hnT[:, k, :],
                                   start=(k == 0), stop=(k == KD - 1))
                mm.then_inc(conv_ps, 1)
                if j == 9:
                    pe.wait_ge(dt_dve, 3)
                    pe.wait_ge(small_ok, 1)
                    for t in range(3):
                        n = P if t < 2 else N_META
                        pe.matmul(bank(0)[:, 32 * t:32 * t + 32], tri_le[0:n, :], adt[0:n, t, :], start=True, stop=True)
                        mm = pe.matmul(bank(0)[:, 96 + 32 * t:128 + 32 * t], ones[0:n, :], adt[0:n, t, :], start=True, stop=True)
                    mm.then_inc(acs_ps, 1)

            def abc(g, t, hf):
                n = 4 * g + 2 * t + hf
                if n >= 2:
                    pe.wait_ge(arg_ok, n - 1)
                for q in range(4):
                    h = GH * g + 4 * hf + q
                    mm = pe.matmul(bank(4 + hf)[:, P * q:P * q + P], adt[:, t, h:h + 1].broadcast_to([P, P]), tri_le,
                                   start=True, stop=True)
                mm.then_inc(abc_ps, 1)

            def z_proj(g, t):
                if g or t:
                    pe.wait_ge(z_used, 2 * g + t)
                for k in range(KD):
                    mm = pe.matmul(bank(7), hnT[:, k, real(t)], wslot(f"Z{g}")[:, k, :], start=(k == 0), stop=(k == KD - 1))
                mm.then_inc(z_ps, 1)

            def y_diag(g, t):
                pe.wait_ge(decay_ok, 4 * g + 2 * t + 2)
                pe.wait_ge(pool_x, 6 * g + (1 if t == 0 else 4))
                if g or t:
                    pe.wait_ge(y_read, 2 * g + t)
                for q in range(GH):
                    mm = pe.matmul(bank(6)[:, HD * q:HD * q + HD], argm[:, q // 4, P * (q % 4):P * (q % 4) + P],
                                   xdt[:, t, HD * q:HD * q + HD], start=True, stop=True)
                mm.then_inc(yd_ps, 1)

            def y_turn(g):
                for t in range(RT):
                    pe.wait_ge(yn_ok, 2 * g + t + 1)
                    for j in range(4):
                        mm = turn(bank(t)[:, P * j:P * j + P], yrow[:, t, P * j:P * j + P])
                    mm.then_inc(yT_ps, 1)

            pe.wait_ge(xbc_ok, CONV_TILES)
            for g in range(GROUPS):
                if g:
                    pe.wait_ge(y_read, 2 * g)
                for t in range(RT):
                    for j in range(4):
                        mm = turn(bank(t)[:, P * j:P * j + P], xbcT[:, 4 * g + j, real(t)])
                    mm.then_inc(xrow_ps, 1)
                if g:
                    pe.wait_ge(state_ok, 2 * g)
                for j in range(4):
                    mm = turn(bank(2)[0:N_META, P * j:P * j + P], xbcT[:, 4 * g + j, 0:N_META])
                mm.then_inc(xrow_ps, 1)
                if g:
                    pe.wait_ge(cbm_ok, g)
                turn(bank(3)[:, 0:P], xbcT[:, 16 + g, real(0)])
                turn(bank(3)[0:N_META, P:2 * P], xbcT[:, 16 + g, 0:N_META])
                for t in range(RT):
                    mm = pe.matmul(bank(3)[:, 256 + P * t:384 + P * t], xbcT[:, 16 + g, real(t)], xbcT[:, 20 + g, real(t)],
                                   start=True, stop=True)
                mm.then_inc(bcb_ps, 1)
                abc(g, 0, 0)
                abc(g, 0, 1)
                loaded(pe, f"Z{g}")
                z_proj(g, 0)
                if g:
                    pe.wait_ge(xrow_ok, 3 * g + 3)
                    y_turn(g - 1)
                pe.wait_ge(xrow_ok, 3 * g + 3)
                pe.wait_ge(brow_ok, g + 1)
                pe.wait_ge(pool_x, 6 * g + 6)
                pe.matmul(bank(2), br[0:N_META, 1, :], xmdec[0:N_META, :], start=True, stop=True).then_inc(state_ps, 1)
                y_diag(g, 0)
                abc(g, 1, 0)
                abc(g, 1, 1)
                pe.wait_ge(state_ok, 2 * g + 1)
                if g:
                    pe.wait_ge(ssmT_ok, 2 * g)
                pe.matmul(bank(0), xbcT[:, 20 + g, real(0)], prev[:, 0, :], start=True, stop=True).then_inc(yo_ps, 1)
                pe.matmul(bank(2), br[:, 0, :], xdec, start=True, stop=True).then_inc(state_ps, 1)
                z_proj(g, 1)
                y_diag(g, 1)
                pe.wait_ge(state_ok, 2 * g + 2)
                pe.matmul(bank(1), xbcT[:, 20 + g, real(1)], prev[:, 1, :], start=True, stop=True).then_inc(yo_ps, 1)

            step = [0]

            def rows_proj(name, t):
                n = step[0]
                step[0] += 1
                loaded(pe, name)
                if n == 0:
                    pe.wait_ge(y_read, 2 * GROUPS)
                    pe.wait_ge(z_used, 2 * GROUPS)
                    pe.wait_ge(state_ok, 2 * GROUPS)
                if n >= 6:
                    pe.wait_ge(proj_ok, n - 5)
                for k in range(KD):
                    mm = pe.matmul(bank(2 + n % 6), hnT[:, k, real(t)], wslot(name)[:, k, :], start=(k == 0), stop=(k == KD - 1))
                mm.then_inc(proj_ps, 1)

            for name in ("K0", "K1"):
                for t in range(RT):
                    rows_proj(name, t)
                if name == "K0":
                    y_turn(GROUPS - 1)
            for name in ("V0", "V1"):
                for t in range(RT):
                    rows_proj(name, t)
            pe.wait_ge(ssmT_ok, 2 * GROUPS)
            for k in range(KD):
                for i, name in enumerate(("K0", "K1", "V0", "V1")):
                    mm = pe.matmul(bank(0)[32 * i:32 * i + N_META, :], hnT[:, k, 0:N_META], wslot(name)[:, k, :],
                                   start=(k == 0), stop=(k == KD - 1))
            mm.then_inc(kmeta_ps, 1)
            for name in ("Q0", "Q1", "QI"):
                for t in range(RT):
                    rows_proj(name, t)

            pe.wait_ge(kmeta_ok, 1)
            pe.wait_ge(proj_ok, 14)
            m = 0

            def turned(parts):
                nonlocal m
                if m >= 8:
                    pe.wait_ge(turn_ok, m - 7)
                for dst, src in parts:
                    mm = turn(bank(m % 8)[:, dst], src)
                mm.then_inc(turn_ps, 1)
                m += 1

            pe.wait_ge(rope_ok, 2)
            for k in range(KD):
                turned([(slice(0, N_META), kraw[0:N_META, 2, P * k:P * k + P]), (real(0), kraw[:, 0, P * k:P * k + P]),
                        (real(1), kraw[:, 1, P * k:P * k + P])])
            pe.wait_ge(rope_ok, 5)
            turned([(slice(P * t, P * t + P), kidup[:, t, :]) for t in range(RT)])
            for k in range(4):
                turned([(slice(P * t, P * t + P), qiraw[:, t, P * k:P * k + P]) for t in range(RT)])
            for k in range(KD):
                turned([(slice(P * t, P * t + P), qraw[:, t, P * k:P * k + P]) for t in range(RT)])
            pe.wait_ge(turn_ok, m)
            n = 0
            for t in range(RT):
                keys = P * (t + 1)
                for i in range(4):
                    if n >= 3:
                        pe.wait_ge(relu_ok, n - 2)
                    for o in range(2):
                        mm = pe.matmul(bank(2 * (n % 3) + o)[:, 0:keys], qiT[64 * o:64 * o + 64, i, P * t:P * t + P],
                                       kiT[64 * o:64 * o + 64, 0:keys], start=True, stop=True)
                    mm.then_inc(idx_ps, 1)
                    n += 1

            def gate(m):
                name = f"G{m // 4}"
                loaded(pe, name)
                if m >= 2:
                    pe.wait_ge(gate_ok, m - 1)
                for k in range(KD):
                    mm = pe.matmul(bank(6 + m % 2)[:, 0:SEQ], wslot(name)[:, k, P * (m % 4):P * (m % 4) + P], hnT[:, k, N_META:T_ALL],
                                   start=(k == 0), stop=(k == KD - 1))
                mm.then_inc(gate_ps, 1)

            def scores(h):
                if h >= 2:
                    pe.wait_ge(s_ok, h - 1)
                o, k = 64 * (h % 2), h // 2
                pe.matmul(bank(h % 2)[:, 0:N_META + P], qT[o:o + 64, k, 0:P], kT[o:o + 64, k, 0:N_META + P], start=True, stop=True)
                pe.matmul(bank(h % 2)[:, N_META + P:416], qT[o:o + 64, k, P:SEQ], kT[o:o + 64, k, :],
                          start=True, stop=True).then_inc(s_ps, 1)

            def turn_probs(h):
                pe.wait_ge(prob_ok, h + 1)
                if h >= 1:
                    pe.wait_ge(pTm_ok, h)
                if h >= 2:
                    pe.wait_ge(pTk_ok, h - 1)
                p = prob[:, h % 2]
                turn(bank(4)[0:N_META, 0:P], p[:, 0:N_META])
                turn(bank(4)[0:N_META, P:2 * P], p[:, 144:160])
                for i, at in enumerate((16, 160, 288)):
                    mm = turn(bank(2 + h % 2)[:, P * i:P * i + P], p[:, at:at + P])
                mm.then_inc(pT_ps, 1)

            def values(h):
                pe.wait_ge(pTk_ok, h + 1)
                pe.wait_ge(pTm_ok, h + 1)
                if h >= 1:
                    pe.wait_ge(ao_ok, h)
                pk, pm, hc = pT_k[:, h % 2], pT_m[:, h % 2], slice(HD * h, HD * h + HD)
                for t in range(RT):
                    o = bank(5)[:, P * (h % 2) + HD * t:P * (h % 2) + HD * t + HD]
                    pe.matmul(o, pm[0:N_META, P * t:P * t + P], vraw[0:N_META, 2, hc], start=True, stop=False)
                    for s in range(t + 1):
                        i = t + s
                        mm = pe.matmul(o, pk[:, P * i:P * i + P], vraw[:, s, hc], start=False, stop=(s == t))
                mm.then_inc(pv_ps, 1)

            for m in range(3):
                gate(m)
            pe.wait_ge(mask_ok, 1)
            scores(0)
            for h in range(HEADS):
                if h + 1 < HEADS:
                    scores(h + 1)
                if h + 3 < 16:
                    gate(h + 3)
                if h:
                    values(h - 1)
                turn_probs(h)
            values(HEADS - 1)

            def o_proj(parts, rhs, m, ps, done):
                for i, (name, k, r) in enumerate(parts):
                    if k == 0:
                        loaded(pe, name)
                    mm = pe.matmul(bank(ps)[:, 0:SEQ], wslot(name)[:, k, P * (m % 4):P * (m % 4) + P], rhs[:, r, :],
                                   start=(i == 0), stop=(i == len(parts) - 1))
                mm.then_inc(done, 1)

            pe.wait_ge(gate_ok, 16)
            for m in range(8):
                if m >= 2:
                    pe.wait_ge(os_ok, m - 1)
                o_proj([(f"OS{2 * (m // 4) + kk}", k, KD * kk + k) for kk in range(2) for k in range(KD)], ssmT, m, 6 + m % 2, os_ps)
            pe.wait_ge(ao_ok, HEADS)
            for k in range(KD):
                if k >= 4:
                    pe.wait_ge(attnT_ok, k - 3)
                for t in range(RT):
                    mm = turn(bank(k % 4)[:, P * t:P * t + P], ao[:, t, P * k:P * k + P])
                mm.then_inc(aoT_ps, 1)
            pe.wait_ge(attnT_ok, KD)
            for m in range(8):
                if m >= 2:
                    pe.wait_ge(uT_ok, m - 1)
                o_proj([(f"OA{m // 4}", k, k) for k in range(KD)], attnT, m, 4 + m % 2, oa_ps)
            pe.wait_ge(uT_ok, 8)
            for c in range(2):
                for t in range(RT):
                    loaded(pe, f"WO{c}")
                    for k in range(KD):
                        mm = pe.matmul(bank(2 * c + t), gatesT[:, k, P * t:P * t + P], wslot(f"WO{c}")[:, k, :],
                                       start=(k == 0), stop=(k == KD - 1))
                    mm.then_inc(wo_ps, 1)

            pe.wait_ge(hn2_ok, 2)
            for k in range(KD):
                for t in range(RT):
                    mm = turn(bank(k)[:, P * t:P * t + P], hn2[:, t, P * k:P * k + P])
                mm.then_inc(hn2T_ps, 1)
            pe.wait_ge(hn2T_ok, KD)
            pe.wait_ge(late_in, 64)
            for t in range(RT):
                for k in range(KD):
                    mm = pe.matmul(bank(0)[:, 32 * t:32 * t + 32], hn2T[:, k, P * t:P * t + P], w_r[:, k, :],
                                   start=(k == 0), stop=(k == KD - 1))
            mm.then_inc(logit_ps, 1)
            pe.wait_ge(dense_ok, 1)
            pe.matmul(bank(6)[:, 0:32], tri_lt, routed[:, 0, :], start=True, stop=True)
            pe.matmul(bank(6)[:, 32:64], ones, routed[:, 0, :], start=True, stop=False)
            pe.matmul(bank(6)[:, 32:64], tri_lt, routed[:, 1, :], start=False, stop=True)
            for t in range(RT):
                mm = pe.matmul(bank(6)[:, 64:96], ones, routed[:, t, :], start=(t == 0), stop=(t == 1))
            for t in range(RT):
                mm = turn(bank(7)[0:EXPERTS, P * t:P * t + P], dense_w[:, t, :])
            mm.then_inc(route_ps, 1)
            pe.wait_ge(dwT_ok, 1)
            for t in range(RT):
                for c in range(2):
                    mm = pe.matmul(bank(2 * t + c), dwT[0:EXPERTS, t, :], bdn[0:EXPERTS, 512 * c:512 * c + 512],
                                   start=True, stop=False, skip_group_check=True)
            mm.then_inc(scat_ps, 1)
            pe.wait_ge(route_ok, 1)

            quarters = [(b, a) for b in range(2) for a in range(2)]

            def gather(u):
                pe.wait_ge(sel_ok, u + 1)
                for t in range(RT):
                    for c in range(2):
                        mm = pe.matmul(bank(6)[64 * c:64 * c + 64, :], sel[:, t, :], hn2[:, t, 512 * c:512 * c + 512],
                                       start=(t == 0), stop=(t == RT - 1))
                mm.then_inc(xrow_ps2, 1)

            def turn_tokens(u):
                pe.wait_ge(xrow_sb, u + 1)
                for j in range(4):
                    mm = turn(bank(5)[:, P * j:P * j + P], xrow[:, P * j:P * j + P])
                mm.then_inc(xe_ps, 1)

            def start_bias(u):
                pe.wait_ge(xe_ok, u + 1)
                pe.wait_ge(hot_ok, u + 1)
                for b, a in quarters:
                    mm = pe.matmul(bank(4 + b)[64 * a:64 * a + 64, :], one_expert[0:96, :],
                                   bias_parts[0:96, FF * b + 512 * a:FF * b + 512 * a + 512], start=True, stop=False)
                mm.then_inc(bias_ps, 1)

            def gate_up(u):
                for k in range(KD):
                    pe.wait_ge(gu_in[k], u * 16 + 16)
                    for b, a in quarters:
                        mm = pe.matmul(bank(4 + b)[64 * a:64 * a + 64, :], xe[:, 2 * (k % 4) + k // 4, :],
                                       gu_chunk[k][:, FF * b + 512 * a:FF * b + 512 * a + 512], start=False, stop=(k == KD - 1))
                    mm.then_inc(gu_free, 1)

            def turn_selection(u):
                pe.wait_ge(selw_ok, u + 1)
                for t in range(RT):
                    mm = turn(bank(7)[:, P * t:P * t + P], selw[:, t, :])
                mm.then_inc(selT_ps, 1)

            def turn_act(u):
                pe.wait_ge(act_ok, u + 1)
                for j in range(4):
                    mm = turn(bank(4)[:, P * j:P * j + P], act[:, P * j:P * j + P])
                mm.then_inc(actT_ps, 1)

            def down(u):
                pe.wait_ge(actT_ok, u + 1)
                pe.wait_ge(selT_ok, u + 1)
                for kk in range(KD):
                    a, j = kk // 4, kk % 4
                    if kk % 2 == 0:
                        pe.wait_ge(dn_in[kk // 2], u * 16 + 16)
                    for c in range(2):
                        mm = pe.matmul(bank(7)[64 * c:64 * c + 64, :], actT[:, P * j + SLOTS * a:P * j + SLOTS * a + SLOTS],
                                       dn_chunk[kk][:, 512 * c:512 * c + 512], start=(kk == 0), stop=(kk == KD - 1))
                    if kk % 2:
                        mm.then_inc(dn_free, 1)

            def scatter(u):
                pe.wait_ge(ysb_ok, u + 1)
                for t in range(RT):
                    for c in range(2):
                        mm = pe.matmul(bank(2 * t + c), selT[64 * c:64 * c + 64, P * t:P * t + P], y_sb[64 * c:64 * c + 64, :],
                                       start=False, stop=False, skip_group_check=True)
                mm.then_inc(scat_ps, 1)

            def prepare(u):
                gather(u)
                turn_tokens(u)
                start_bias(u)

            def unit(u, ahead):
                gate_up(u)
                turn_selection(u)
                if ahead:
                    gather(u + 1)
                turn_act(u)
                if ahead:
                    turn_tokens(u + 1)
                down(u)
                if ahead:
                    start_bias(u + 1)
                scatter(u)

            pe.wait_ge(bias_part, 6)
            prepare(0)
            with pe.Fori(0, EXPERTS - 1) as u:
                unit(u, True)
            unit(EXPERTS - 1, False)
            over = pe.value_load(n_over[0:1, 0:1], min_val=0, max_val=OVERFLOW_MAX)
            with pe.If(over > 0):
                with pe.Fori(0, over) as j:
                    prepare(j + EXPERTS)
                    unit(j + EXPERTS, False)

        @block.scalar
        def _(act_e):
            chain = [0]

            def link(ins):
                chain[0] += 1
                ins.then_inc(act_chain, 1)
                act_e.wait_ge(act_chain, chain[0])

            def act_f(o, i, f, **kw):
                return nc.scalar.activation(o, i, f, **kw)

            def copy(o, i):
                return nc.scalar.activation(o, i, ACT.Copy)

            act_e.dma_start(const[:, :], const_dram[:, :]).then_inc(const_in, 16)
            act_e.dma_start(rows1[0:96, :], conv_w[0].rearrange("w (j p) -> (w j) p", p=P)).then_inc(rows_in, 16)
            act_e.dma_start(rows1[96:120, :], conv_b[0].rearrange("(j p) -> j p", p=P)).then_inc(rows_in, 16)
            act_e.dma_start(rows1[120:128, :], norm1_g[0].rearrange("(j p) -> j p", p=P)).then_inc(rows_in, 16)
            act_e.dma_start(rows2[0:16, :], ssm_norm_g[0].rearrange("(j p) -> j p", p=P)).then_inc(rows_in, 16)
            act_e.dma_start(rows2[16:24, :], norm2_g[0].rearrange("(j p) -> j p", p=P)).then_inc(rows_in, 16)
            for i, v in enumerate((dt_bias, a_log, d_skip)):
                act_e.dma_start(bc[:, i, :], v[0].partition_broadcast(P)).then_inc(vec_in, 16)
            act_e.wait_ge(zeroed, 2)
            act_e.wait_ge(x_in, 32)
            for t in range(3):
                n = P if t < 2 else N_META
                src = hrow[:, t, :] if t < 2 else hmeta[0:n, :]
                i = act_f(xn[0:n, t, :], src, ACT.Square, accum_out=stat[0:n, t:t + 1])
            i.then_inc(sq1, 1)
            act_e.wait_ge(sq1, 2)
            act_f(stat[:, 3:6], stat[:, 3:6], ACT.Sqrt).then_inc(rstd1, 1)
            act_e.wait_ge(small_ps, 1)
            copy(small[:, 0:2, :].rearrange("p t c -> p (t c)"), bank(0)[:, 0:208])
            copy(small[0:N_META, 2, :], bank(0)[0:N_META, 208:312]).then_inc(small_ok, 1)
            act_e.wait_ge(dt_dve, 1)
            link(act_f(dt_e, dt_n, ACT.Exp))
            act_e.wait_ge(vec_in, 48)
            act_f(ea_log, bc[:, 1, :], ACT.Exp)
            act_f(dt_l, dt_e, ACT.Ln, bias=ones[:, 0:1]).then_inc(dt_act, 1)

            for j in range(CONV_TILES):
                act_e.wait_ge(conv_ok, j + 1)
                act_f(xbcT[:, j, :], conv_acc[:, j % 3, :], ACT.Silu, bias=convb_col[j]).then_inc(xbc_ok, 1)
                if j == 11:
                    act_e.wait_ge(acs_ps, 1)
                    copy(acs.rearrange("p a b -> p (a b)"), bank(0)[:, 0:192]).then_inc(dt_act, 1)
            act_e.wait_ge(dt_dve, 4)
            act_e.wait_ge(dt_act, 2)
            act_f(eacs, acs[:, 0:2, :], ACT.Exp)
            act_f(cdec, acs[:, 3, :], ACT.Exp)
            act_f(wdec, wdec, ACT.Exp).then_inc(dt_act, 1)

            def y_square(g, t):
                act_e.wait_ge(y_ok, 2 * g + t + 1)
                link(act_f(square_junk, yrow[:, t, :], ACT.Square, accum_out=ss_y[:, 2 * (g % 4) + t:2 * (g % 4) + t + 1]))
                act_e.wait_ge(act_chain, chain[0])
                act_f(ss_y[:, 8 + 2 * g + t:9 + 2 * g + t], ss_y[:, 2 * g + t:2 * g + t + 1], ACT.Sqrt,
                      scale=1.0 / 512, bias=stat[:, 8:9]).then_inc(ysq_ok, 1)

            for g in range(GROUPS):
                for t in range(RT):
                    act_e.wait_ge(xrow_ps, 3 * g + t + 1)
                    if g:
                        act_e.wait_ge(pool_x, 6 * g)
                    copy(xr[:, t, :], bank(t)).then_inc(xrow_ok, 1)
                act_e.wait_ge(xrow_ps, 3 * g + 3)
                copy(xm[0:N_META, :], bank(2)[0:N_META, :]).then_inc(xrow_ok, 1)
                act_e.wait_ge(bcb_ps, g + 1)
                copy(br[:, 0, :], bank(3)[:, 0:P])
                copy(br[0:N_META, 1, :], bank(3)[0:N_META, P:2 * P]).then_inc(brow_ok, 1)
                for t in range(RT):
                    for hf in range(2):
                        act_e.wait_ge(arg_ok, 4 * g + 2 * t + hf + 1)
                        act_f(argm[:, hf, :], argm[:, hf, :], ACT.Exp).then_inc(exp_ok, 1)
                    if t == 0:
                        act_e.wait_ge(state_ps, 2 * g + 1)
                        copy(prev[:, 0, :], bank(2)).then_inc(state_ok, 1)
                    act_e.wait_ge(z_ps, 2 * g + t + 1)
                    act_f(tanh_z, bank(7), ACT.Tanh, scale=0.5).then_inc(tanh_ok, 1)
                    if t:
                        for tt in range(RT):
                            y_square(g, tt)

            dst = [kraw[:, t, 512 * c:512 * c + 512] for c in range(2) for t in range(RT)] \
                + [vraw[:, t, 512 * c:512 * c + 512] for c in range(2) for t in range(RT)]
            for n, d in enumerate(dst):
                act_e.wait_ge(proj_ps, n + 1)
                if n == 0:
                    act_e.wait_ge(ssmT_ok, 2 * GROUPS)
                copy(d, bank(2 + n % 6)).then_inc(proj_ok, 1)
            act_e.wait_ge(kmeta_ps, 1)
            copy(kraw[0:N_META, 2, 0:512], bank(0)[0:N_META, :])
            copy(kraw[0:N_META, 2, 512:D], bank(0)[32:32 + N_META, :])
            copy(vraw[0:N_META, 2, 0:512], bank(0)[64:64 + N_META, :])
            copy(vraw[0:N_META, 2, 512:D], bank(0)[96:96 + N_META, :]).then_inc(kmeta_ok, 1)
            dst = [qraw[:, t, 512 * c:512 * c + 512] for c in range(2) for t in range(RT)] + [qiraw[:, t, :] for t in range(RT)]
            for n, d in enumerate(dst):
                act_e.wait_ge(proj_ps, 8 + n + 1)
                copy(d, bank(2 + (8 + n) % 6)).then_inc(proj_ok, 1)
            dst = [kT[:, k, :] for k in range(KD)] + [kiT] + [qiT[:, k, :] for k in range(4)] + [qT[:, k, :] for k in range(KD)]
            for n, d in enumerate(dst):
                act_e.wait_ge(turn_ps, n + 1)
                copy(d, bank(n % 8)[:, 0:d.shape[1]]).then_inc(turn_ok, 1)
            for n in range(8):
                act_e.wait_ge(idx_ps, n + 1)
                if n >= 2:
                    act_e.wait_ge(relu_used, n - 1)
                keys = P if n < 4 else SEQ
                act_f(split(relu_b[:, n % 2, 0:2 * keys], 2), PS[:, 2 * (n % 3):2 * (n % 3) + 2, 0:keys], ACT.Relu, scale=HD ** -0.5).then_inc(relu_ok, 1)

            def gate_copy(m):
                act_e.wait_ge(gate_ps, m + 1)
                copy(gatesT[:, m, :], bank(6 + m % 2)[:, 0:SEQ]).then_inc(gate_ok, 1)

            for m in range(3):
                gate_copy(m)
            for h in range(HEADS):
                act_e.wait_ge(s_ok, h + 1)
                if h >= 2:
                    act_e.wait_ge(pT_ps, h - 1)
                st = head_stat[:, h % 4]
                act_f(prob[:, h % 2, 0:144], sbuf_s[:, h % 2, 0:144], ACT.Exp, scale=HD ** -0.5, bias=st[:, 2:3], accum_out=st[:, 4:5])
                act_f(prob[:, h % 2, 144:416], sbuf_s[:, h % 2, 144:416], ACT.Exp, scale=HD ** -0.5, bias=st[:, 3:4],
                      accum_out=st[:, 5:6]).then_inc(prob_ok, 1)
                if h + 3 < 16:
                    gate_copy(h + 3)
                act_e.wait_ge(pT_ps, h + 1)
                if h >= 2:
                    act_e.wait_ge(pv_ps, h - 1)
                copy(pT_m[0:N_META, h % 2, :], bank(4)[0:N_META, 0:256]).then_inc(pTm_ok, 1)
                copy(pT_k[:, h % 2, :], bank(2 + h % 2)[:, 0:384]).then_inc(pTk_ok, 1)
            act_e.wait_ge(gate_ok, 16)
            act_f(gatesT[:, 8:16, :], gatesT[:, 8:16, :], ACT.Sigmoid).then_inc(sigm_ok, 1)
            act_f(gatesT[:, 0:8, :], gatesT[:, 0:8, :], ACT.Sigmoid).then_inc(sigm_ok, 1)
            for k in range(KD):
                act_e.wait_ge(aoT_ps, k + 1)
                copy(attnT[:, k, :], bank(k % 4)[:, 0:SEQ]).then_inc(attnT_ok, 1)
            act_e.wait_ge(h2_ok, 4)
            for t in range(RT):
                i = act_f(hn2[:, t, :], hrow[:, t, :], ACT.Square, accum_out=rstat[:, t:t + 1])
            i.then_inc(sq2, 1)
            act_e.wait_ge(sq2, 2)
            act_f(rstat[:, 2:4], rstat[:, 2:4], ACT.Sqrt).then_inc(rstd2, 1)
            for k in range(1, KD, 2):
                act_e.wait_ge(hn2T_ps, k + 1)
                act_f(hn2T[:, k, :], bank(k)[:, 0:SEQ], ACT.Copy, scale=g2_cols[:, k:k + 1]).then_inc(hn2T_ok, 1)
            act_e.wait_ge(negv_ok, 1)
            for t in range(RT):
                i = act_f(e4[:, t, 0:4], v8[:, t, 0:4], ACT.Exp, bias=rstat[:, 4 + t:5 + t], accum_out=rstat[:, 6 + t:7 + t])
            i.then_inc(e4_ok, 1)
            act_e.wait_ge(route_ps, 1)
            copy(dwT[0:EXPERTS].rearrange("p a b -> p (a b)"), bank(7)[0:EXPERTS, 0:256]).then_inc(dwT_ok, 1)

            def tokens_out(u):
                act_e.wait_ge(xrow_ps2, u + 1)
                copy(xrow, bank(6)).then_inc(xrow_sb, 1)

            def unit(u, ahead):
                act_e.wait_ge(selT_ps, u + 1)
                act_e.wait_ge(scat_ps, u + 1)
                copy(selT, bank(7)[:, 0:256]).then_inc(selT_ok, 1)
                act_e.wait_ge(gmin_ok, u + 1)
                act_f(sig, gmin, ACT.Sigmoid, scale=ALPHA).then_inc(sig_ok, 1)
                if ahead:
                    tokens_out(u + 1)
                act_e.wait_ge(actT_ps, u + 1)
                copy(actT, bank(4)).then_inc(actT_ok, 1)
                act_e.wait_ge(dn_free, u * 4 + 4)
                copy(y_sb, bank(7)).then_inc(ysb_ok, 1)

            act_f(stat[:, 9:10], stat[:, 8:9], ACT.Sigmoid)
            tokens_out(0)
            with act_e.Fori(0, EXPERTS - 1) as u:
                unit(u, True)
            unit(EXPERTS - 1, False)
            act_e.wait_ge(route_ok, 1)
            over = act_e.value_load(n_over[0:1, 0:1], min_val=0, max_val=OVERFLOW_MAX)
            with act_e.If(over > 0):
                with act_e.Fori(0, over) as j:
                    tokens_out(j + EXPERTS)
                    unit(j + EXPERTS, False)
            for t in range(RT):
                act_e.wait_ge(sum_ok, t + 1)
                i = act_f(final[:, t, :], hrow[:, t, :], ACT.Square, accum_out=rstat[:, 8 + t:9 + t])
            i.then_inc(sq3, 1)
            act_e.wait_ge(sq3, 2)
            act_f(rstat[:, 10:12], rstat[:, 10:12], ACT.Sqrt).then_inc(sq3, 1)

        @block.vector
        def _(dve):
            V = nc.vector
            chain = [0]

            def link(ins):
                chain[0] += 1
                ins.then_inc(dve_chain, 1)
                dve.wait_ge(dve_chain, chain[0])

            V.memset(small_t[:, 208:312], 0.0).then_inc(zeroed, 1)
            V.memset(stat[:, 8:9], EPS)
            V.memset(stat[:, 0:6], 1.0).then_inc(zeroed, 1)
            dve.wait_ge(sq1, 1)
            V.tensor_scalar(stat[:, 3:6], stat[:, 0:3], 1.0 / D, EPS, ALU.mult, ALU.add).then_inc(sq1, 1)
            dve.wait_ge(rstd1, 1)
            link(V.reciprocal(stat[:, 3:6], stat[:, 3:6]))
            for t in range(3):
                n = P if t < 2 else N_META
                src = hrow[:, t, :] if t < 2 else hmeta[0:n, :]
                V.tensor_scalar(xn[0:n, t, :], src, stat[0:n, 3 + t:4 + t], None, ALU.mult).then_inc(xn_ok, 1)
            dve.wait_ge(cols_ps, 1)
            V.tensor_copy(cols1[:, :], bank(0)[:, 0:P])
            V.tensor_copy(cols2[:, :], bank(0)[:, P:P + 24]).then_inc(cols_ok, 1)
            dve.wait_ge(cols_ok, 1)
            for k in range(KD):
                dve.wait_ge(xnT_ps, k + 1)
                V.tensor_scalar(hnT[:, k, :], bank(k)[:, 0:T_ALL], g1_col[k], None, ALU.mult).then_inc(hnT_ok, 1)
            dve.wait_ge(small_ok, 1)
            dve.wait_ge(vec_in, 48)
            link(V.tensor_tensor(dt_x, small[:, :, 72:104], bc[:, 0, :].unsqueeze(1).broadcast_to([P, 3, 32]), ALU.add))
            V.scalar_tensor_tensor(out=dt_n, in0=dt_x, scalar=-1.0, in1=dt_x, op0=ALU.mult, op1=ALU.min).then_inc(dt_dve, 1)

            def conv(j):
                dve.wait_ge(conv_ps, j + 1)
                if j >= 3:
                    dve.wait_ge(xbc_ok, j - 2)
                ps, ca = bank(1 + j % 7), conv_acc[:, j % 3, :]
                link(V.tensor_scalar(ca, ps[:, 0:T_ALL], conv_col[3][j], None, ALU.mult))
                for back in range(1, CONV_W):
                    i = V.scalar_tensor_tensor(out=ca[:, back:], in0=ps[:, 0:T_ALL - back], scalar=conv_col[3 - back][j],
                                               in1=ca[:, back:], op0=ALU.mult, op1=ALU.add)
                    if back < CONV_W - 1:
                        link(i)
                i.then_inc(conv_ok, 1)

            for j in range(CONV_TILES):
                conv(j)
                if j == 1:
                    dve.wait_ge(dt_act, 1)
                    V.scalar_tensor_tensor(out=dtv, in0=dt_x, scalar=0.0, in1=dt_l, op0=ALU.max, op1=ALU.add).then_inc(dt_dve, 1)
                    dve.wait_ge(dt_dve, 2)
                    V.scalar_tensor_tensor(out=adt, in0=dtv, scalar=-1.0, in1=ea_log.unsqueeze(1).broadcast_to([P, 3, 32]),
                                           op0=ALU.mult, op1=ALU.mult).then_inc(dt_dve, 1)
                if j == 14:
                    dve.wait_ge(dt_act, 2)
                    V.tensor_tensor(wdec, acs[:, 3:6, :], acs[:, 0:3, :], ALU.subtract).then_inc(dt_dve, 1)
            dve.wait_ge(dt_act, 3)
            V.tensor_tensor(wdec, wdec, dtv, ALU.mult).then_inc(dt_dve, 1)

            def per_head(v):
                return v.unsqueeze(2).broadcast_to([P, GH, HD])

            def heads(v):
                return v.rearrange("p (h e) -> p h e", h=GH)

            def decay_args(g, t):
                for hf in range(2):
                    n = 4 * g + 2 * t + hf
                    dve.wait_ge(abc_ps, n + 1)
                    if n >= 2:
                        dve.wait_ge(yd_ps, 2 * g + t)
                    for q in range(4):
                        h = GH * g + 4 * hf + q
                        i = V.tensor_scalar(argm[:, hf, P * q:P * q + P], bank(4 + hf)[:, P * q:P * q + P], acs[:, t, h:h + 1], 0.0,
                                            ALU.subtract, ALU.min)
                    i.then_inc(arg_ok, 1)

            def decay_times_cb(g, t):
                for hf in range(2):
                    dve.wait_ge(exp_ok, 4 * g + 2 * t + hf + 1)
                    V.tensor_tensor(split(argm[:, hf, :], 4), split(argm[:, hf, :], 4),
                                    cbm[:, t, :].unsqueeze(1).broadcast_to([P, 4, P]), ALU.mult).then_inc(decay_ok, 1)

            def y_sum(g, t):
                hs = slice(GH * g, GH * g + GH)
                dve.wait_ge(tanh_ok, 2 * g + t + 1)
                V.scalar_tensor_tensor(out=gated, in0=tanh_z, scalar=1.0, in1=bank(7), op0=ALU.add, op1=ALU.mult).then_inc(z_used, 1)
                dve.wait_ge(yo_ps, 2 * g + t + 1)
                if g:
                    dve.wait_ge(yT_ps, 2 * g)
                link(V.tensor_tensor(heads(yrow[:, t, :]), heads(bank(t)), per_head(eacs[:, t, hs]), ALU.mult))
                dve.wait_ge(yd_ps, 2 * g + t + 1)
                i = V.tensor_tensor(yrow[:, t, :], yrow[:, t, :], bank(6), ALU.add)
                i.then_inc(y_read, 1)
                dve.wait_ge(y_read, 2 * g + t + 1)
                dve.wait_ge(pool_x, 6 * g + (2 if t == 0 else 5))
                link(V.tensor_tensor(yrow[:, t, :], yrow[:, t, :], xsk[:, t, :], ALU.add))
                dve.wait_ge(z_used, 2 * g + t + 1)
                V.scalar_tensor_tensor(out=yrow[:, t, :], in0=yrow[:, t, :], scalar=0.5, in1=gated, op0=ALU.mult, op1=ALU.mult)\
                 .then_inc(y_ok, 1)

            def y_norm(g):
                for t in range(RT):
                    dve.wait_ge(ysq_ok, 2 * g + t + 1)
                    r = ss_y[:, 8 + 2 * g + t:9 + 2 * g + t]
                    link(V.reciprocal(r, r))
                    V.tensor_scalar(yrow[:, t, :], yrow[:, t, :], r, None, ALU.mult).then_inc(yn_ok, 1)

            def y_store(g):
                for t in range(RT):
                    dve.wait_ge(yT_ps, 2 * g + t + 1)
                    V.tensor_tensor(ssmT[:, 4 * g:4 * g + 4, P * t:P * t + P], split(bank(t), 4),
                                    ssmg_cols[:, 4 * g:4 * g + 4].unsqueeze(2).broadcast_to([P, 4, P]), ALU.mult).then_inc(ssmT_ok, 1)

            for g in range(GROUPS):
                hs = slice(GH * g, GH * g + GH)
                dve.wait_ge(brow_ok, g + 1)
                V.tensor_tensor(cbm, split(bank(3)[:, 256:512], 2), tri_le.unsqueeze(1).broadcast_to([P, 2, P]), ALU.mult)\
                 .then_inc(cbm_ok, 1)
                decay_args(g, 0)
                if g:
                    y_store(g - 1)
                dve.wait_ge(cbm_ok, g + 1)
                decay_times_cb(g, 0)
                decay_args(g, 1)
                y_sum(g, 0)
                dve.wait_ge(state_ok, 2 * g + 1)
                link(V.tensor_tensor(heads(prev[:, 1, :]), heads(prev[:, 0, :]), per_head(cdec[:, hs]), ALU.mult))
                dve.wait_ge(state_ps, 2 * g + 2)
                V.tensor_tensor(prev[:, 1, :], prev[:, 1, :], bank(2), ALU.add).then_inc(state_ok, 1)
                decay_times_cb(g, 1)
                y_sum(g, 1)
                y_norm(g)
            y_store(GROUPS - 1)

            def rope(v, tiles, n_heads, tab):
                p = v.shape[0]
                v4 = v.rearrange("p t (h e) -> p t h e", h=n_heads)
                a, b = v4[:, :, :, 0:HALF], v4[:, :, :, HALF:ROT]
                cos, sin = (tab[:, :, c:c + HALF].unsqueeze(2).broadcast_to([p, tiles, n_heads, HALF]) for c in (0, HALF))
                tmp = [rope_tmp[0:p, i, 0:tiles * n_heads * HALF].rearrange("p (t h e) -> p t h e", t=tiles, h=n_heads) for i in range(4)]
                V.tensor_tensor(tmp[0], a, cos, ALU.mult)
                V.tensor_tensor(tmp[1], b, sin, ALU.mult)
                V.tensor_tensor(tmp[2], b, cos, ALU.mult)
                link(V.tensor_tensor(tmp[3], a, sin, ALU.mult))
                V.tensor_tensor(a, tmp[0], tmp[1], ALU.subtract)
                V.tensor_tensor(b, tmp[2], tmp[3], ALU.add).then_inc(rope_ok, 1)
                dve.wait_ge(rope_ok, ropes[0] + 1)
                ropes[0] += 1

            ropes = [0]
            dve.wait_ge(proj_ok, 4)
            rope(kraw[:, 0:2, :], 2, HEADS, rope_tab[:, 0:2, :])
            dve.wait_ge(kmeta_ok, 1)
            rope(kraw[0:N_META, 2:3, :], 1, HEADS, rope_tab[0:N_META, 2:3, :])
            rope(small[:, 0:2, 0:64], 2, 1, rope_tab[:, 0:2, :])
            V.tensor_copy(kidup[:, :, 0:64], small[:, 0:2, 0:64])
            V.tensor_copy(kidup[:, :, 64:128], small[:, 0:2, 0:64])
            V.tensor_scalar(small[:, 0:2, 64:72], small[:, 0:2, 64:72], IDX_HEADS ** -0.5, None, ALU.mult)
            dve.wait_ge(proj_ok, 12)
            rope(qraw, 2, HEADS, rope_tab[:, 0:2, :])
            dve.wait_ge(proj_ok, 14)
            rope(qiraw, 2, IDX_HEADS, rope_tab[:, 0:2, :])

            n = 0
            for t in range(RT):
                keys = P * (t + 1)
                for i in range(4):
                    dve.wait_ge(relu_ok, n + 1)
                    for o in range(2):
                        w = small[:, t, 64 + 2 * i + o:65 + 2 * i + o]
                        r = relu_b[:, n % 2, keys * o:keys * o + keys]
                        if i == 0 and o == 0:
                            link(V.tensor_scalar(score[:, t, 0:keys], r, w, None, ALU.mult))
                        else:
                            j = V.scalar_tensor_tensor(out=score[:, t, 0:keys], in0=r, scalar=w, in1=score[:, t, 0:keys],
                                                       op0=ALU.mult, op1=ALU.add)
                            if o:
                                j.then_inc(relu_used, 1)
                                dve.wait_ge(relu_used, n + 1)
                            else:
                                link(j)
                    n += 1
            for t in range(RT):
                keys = P * (t + 1)
                if t:
                    V.tensor_copy(work[:, t, 0:P], score[:, t, 0:P])
                link(V.tensor_tensor(work[:, t, keys - P:keys], score[:, t, keys - P:keys], cst("causal_neg"), ALU.add))
            for r in range(TOPK_KEYS // 8):
                for t in range(RT):
                    keys = P * (t + 1)
                    j = V.max(top8[:, 64 * t + 8 * r:64 * t + 8 * r + 8], work[:, t, 0:keys])
                link(j)
                for t in range(RT):
                    keys = P * (t + 1)
                    j = V.match_replace(work[:, t, 0:keys], top8[:, 64 * t + 8 * r:64 * t + 8 * r + 8], work[:, t, 0:keys], PICKED)
                link(j)
            V.memset(amask[:, 0:N_META], 0.0)
            V.memset(amask[:, 144:160], 0.0)
            am = [amask[:, 16:144], amask[:, 160:416]]
            for t in range(RT):
                keys = P * (t + 1)
                j = V.tensor_scalar(am[t], work[:, t, 0:keys], PICKED, None, ALU.is_equal)
            link(j)
            for t in range(RT):
                j = V.tensor_tensor(am[t][:, P * t:P * t + P], am[t][:, P * t:P * t + P], cst("causal"), ALU.mult)
            link(j)
            for t in range(RT):
                j = V.tensor_scalar(am[t], am[t], 1.0, 1.0e30, ALU.subtract, ALU.mult)
            j.then_inc(mask_ok, 1)
            dve.wait_ge(mask_ok, 1)

            def head_scores(h):
                dve.wait_ge(s_ps, h + 1)
                if h >= 2:
                    dve.wait_ge(prob_ok, h - 1)
                st, s = head_stat[:, h % 4], sbuf_s[:, h % 2, :]
                link(V.tensor_tensor(s, bank(h % 2)[:, 0:416], amask, ALU.add))
                V.tensor_reduce(st[:, 0:1], s[:, 0:144], AX.X, ALU.max)
                link(V.tensor_reduce(st[:, 1:2], s[:, 144:416], AX.X, ALU.max))
                V.tensor_scalar(st[:, 2:4], st[:, 0:2], -(HD ** -0.5), None, ALU.mult).then_inc(s_ok, 1)

            def head_out(h):
                dve.wait_ge(prob_ok, h + 1)
                st = head_stat[:, h % 4]
                link(V.reciprocal(st[:, 6:8], st[:, 4:6]))
                dve.wait_ge(pv_ps, h + 1)
                for t in range(RT):
                    j = V.tensor_scalar(ao[:, t, HD * h:HD * h + HD], bank(5)[:, P * (h % 2) + HD * t:P * (h % 2) + HD * t + HD],
                                        st[:, 6 + t:7 + t], None, ALU.mult)
                j.then_inc(ao_ok, 1)

            head_scores(0)
            for h in range(HEADS):
                if h + 1 < HEADS:
                    head_scores(h + 1)
                if h:
                    head_out(h - 1)
            head_out(HEADS - 1)
            dve.wait_ge(sigm_ok, 1)
            for m in range(8):
                dve.wait_ge(os_ps, m + 1)
                V.tensor_tensor(gatesT[:, 8 + m, :], bank(6 + m % 2)[:, 0:SEQ], gatesT[:, 8 + m, :], ALU.mult).then_inc(os_ok, 1)
            dve.wait_ge(sigm_ok, 2)
            dve.wait_ge(os_ok, 8)
            for m in range(8):
                dve.wait_ge(oa_ps, m + 1)
                link(V.tensor_tensor(gatesT[:, m, :], bank(4 + m % 2)[:, 0:SEQ], gatesT[:, m, :], ALU.mult))
                V.tensor_tensor(gatesT[:, m, :], gatesT[:, m, :], gatesT[:, 8 + m, :], ALU.add).then_inc(uT_ok, 1)
            for n in range(4):
                c, t = n // 2, n % 2
                dve.wait_ge(wo_ps, n + 1)
                V.tensor_tensor(hrow[:, t, 512 * c:512 * c + 512], bank(2 * c + t), hrow[:, t, 512 * c:512 * c + 512], ALU.add)\
                 .then_inc(h2_ok, 1)

            dve.wait_ge(sq2, 1)
            V.tensor_scalar(rstat[:, 2:4], rstat[:, 0:2], 1.0 / D, EPS, ALU.mult, ALU.add).then_inc(sq2, 1)
            dve.wait_ge(rstd2, 1)
            link(V.reciprocal(rstat[:, 2:4], rstat[:, 2:4]))
            for t in range(RT):
                V.tensor_scalar(hn2[:, t, :], hrow[:, t, :], rstat[:, 2 + t:3 + t], None, ALU.mult).then_inc(hn2_ok, 1)
            for k in range(0, KD, 2):
                dve.wait_ge(hn2T_ps, k + 1)
                V.tensor_scalar(hn2T[:, k, :], bank(k)[:, 0:SEQ], g2_cols[:, k:k + 1], None, ALU.mult).then_inc(hn2T_ok, 1)
            dve.wait_ge(logit_ps, 1)
            link(V.tensor_tensor(logit, split(bank(0)[:, 0:64], 2), br_bc.unsqueeze(1).broadcast_to([P, 2, 32]), ALU.add))
            for t in range(RT):
                j = V.max(v8[:, t, :], logit[:, t, :])
            link(j)
            for t in range(RT):
                V.max_index(idx8[:, t, :], v8[:, t, :], logit[:, t, :])
            j = V.tensor_scalar(rstat[:, 4:6], v8[:, :, 0:1].rearrange("p a b -> p (a b)"), -1.0, None, ALU.mult)
            j.then_inc(negv_ok, 1)
            dve.wait_ge(negv_ok, 1)
            V.tensor_copy(idxf, idx8)
            dve.wait_ge(e4_ok, 1)
            link(V.reciprocal(rstat[:, 6:8], rstat[:, 6:8]))
            for t in range(RT):
                j = V.tensor_scalar(w4[:, t, 0:4], e4[:, t, 0:4], rstat[:, 6 + t:7 + t], None, ALU.mult)
            link(j)
            for t in range(RT):
                for i in range(TOP_K):
                    j = V.tensor_scalar(pick[:, t, EXPERTS * i:EXPERTS * i + EXPERTS], cst("experts"), idxf[:, t, i:i + 1],
                                        w4[:, t, i:i + 1], ALU.is_equal, ALU.mult)
            link(j)
            for t in range(RT):
                j = V.tensor_reduce(dense_w[:, t, :], pick[:, t, :].rearrange("p (i e) -> p e i", i=TOP_K), AX.X, ALU.add)
            link(j)
            V.tensor_scalar(routed, dense_w, 0.0, None, ALU.is_gt).then_inc(dense_ok, 1)
            dve.wait_ge(dense_ok, 1)
            dve.wait_ge(route_ps, 1)
            V.tensor_copy(count[0:1, :], bank(6)[0:1, 64:96])
            link(V.scalar_tensor_tensor(out=posm, in0=split(bank(6)[:, 0:64], 2), scalar=UNROUTED, in1=routed, op0=ALU.add, op1=ALU.mult))
            V.tensor_scalar(posm, posm, UNROUTED, None, ALU.subtract)
            link(V.tensor_tensor(split(flags[0:1, :], 3), count[0:1, :].unsqueeze(1).broadcast_to([1, 3, EXPERTS]),
                                 split(cst("thresholds")[0:1, :], 3), ALU.is_gt))
            link(V.tensor_reduce(n_over_f[0:1, :], flags[0:1, :], AX.X, ALU.add))
            V.tensor_copy(n_over[0:1, :], n_over_f[0:1, :]).then_inc(route_ok, 1)
            dve.wait_ge(route_ok, 1)

            def slot_ids(b):
                return slots[:, 0, :] if b is None else slots[:, bass.ds(b, 1), :].rearrange("p b s -> p (b s)")

            def select(u, e, b):
                for t in range(RT):
                    j = V.tensor_scalar(sel[:, t, :], slot_ids(b)[:, 0:SLOTS], posm[:, t, bass.ds(e, 1)], None, ALU.is_equal)
                j.then_inc(sel_ok, 1)
                V.tensor_scalar(one_expert[0:96, :], cst("row_expert")[0:96, :].broadcast_to([96, SLOTS]),
                                cst("experts")[0:96, bass.ds(e, 1)], None, ALU.is_equal).then_inc(hot_ok, 1)

            def tokens_in(u):
                dve.wait_ge(xe_ps, u + 1)
                V.tensor_tensor(xe_flat.rearrange("p (j a s) -> p j a s", j=4, a=2), bank(5).rearrange("p (j a s) -> p j a s", j=4, a=2),
                                g2_cols.rearrange("p (a j) -> p j a", a=2).unsqueeze(3).broadcast_to([P, 4, 2, SLOTS]),
                                ALU.mult).then_inc(xe_ok, 1)

            def unit(u, e, b, ahead):
                for t in range(RT):
                    j = V.tensor_scalar(selw[:, t, :], slot_ids(b), posm[:, t, bass.ds(e, 1)], dense_w[:, t, bass.ds(e, 1)],
                                        ALU.is_equal, ALU.mult)
                j.then_inc(selw_ok, 1)
                if ahead:
                    dve.wait_ge(bias_ps, u + 1)
                    select(u + 1, e + 1, b)
                dve.wait_ge(gu_free, u * KD + KD)
                V.tensor_scalar(gmin, bank(4), LIMIT, None, ALU.min).then_inc(gmin_ok, 1)
                V.tensor_scalar(upc, bank(5), LIMIT, -LIMIT, ALU.min, ALU.max).then_inc(upc_ok, 1)
                dve.wait_ge(gmin_ok, u + 1)
                dve.wait_ge(upc_ok, u + 1)
                V.scalar_tensor_tensor(out=upc, in0=upc, scalar=1.0, in1=gmin, op0=ALU.add, op1=ALU.mult).then_inc(upg_ok, 1)
                dve.wait_ge(upg_ok, u + 1)
                dve.wait_ge(sig_ok, u + 1)
                V.tensor_tensor(act, upc, sig, ALU.mult).then_inc(act_ok, 1)
                if ahead:
                    tokens_in(u + 1)

            select(0, 0, None)
            tokens_in(0)
            with dve.Fori(0, EXPERTS - 1) as u:
                unit(u, u, None, True)
            unit(EXPERTS - 1, EXPERTS - 1, None, False)
            over = dve.value_load(n_over[0:1, 0:1], min_val=0, max_val=OVERFLOW_MAX)
            with dve.If(over > 0):
                link(V.tensor_tensor_scan(seq[0:1, :], ones[0:1, 0:96], flags[0:1, :], 0.0, ALU.mult, ALU.add))
                link(V.tensor_tensor(seq[0:1, :], seq[0:1, :], flags[0:1, :], ALU.mult))
                link(V.tensor_scalar(seq[0:1, :], seq[0:1, :], 1.0, None, ALU.subtract))
                link(V.tensor_tensor(one_hot[0:1], seq[0:1, :].unsqueeze(1).broadcast_to([1, OVERFLOW_MAX, 96]),
                                     cst("turns")[0:1, :].unsqueeze(2).broadcast_to([1, OVERFLOW_MAX, 96]), ALU.is_equal))
                link(V.tensor_tensor(one_hot[0:1], one_hot[0:1], cst("codes")[0:1, :].unsqueeze(1).broadcast_to([1, OVERFLOW_MAX, 96]), ALU.mult))
                link(V.tensor_reduce(codes_f[0:1, :], one_hot[0:1], AX.X, ALU.add))
                V.tensor_copy(codes[0:1, :], codes_f[0:1, :]).then_inc(codes_ok, 1)
                dve.wait_ge(codes_ok, 1)
                with dve.Fori(0, over) as j:
                    jj = nc.s_assert_within(j, 0, OVERFLOW_MAX - 1)
                    code = dve.value_load(codes[0:1, bass.ds(jj, 1)], min_val=0, max_val=4 * EXPERTS - 1)
                    select(jj + EXPERTS, code % EXPERTS, code // EXPERTS)
                    tokens_in(jj + EXPERTS)
                    unit(jj + EXPERTS, code % EXPERTS, code // EXPERTS, False)
                    dve.wait_ge(scat_ps, jj + EXPERTS + 2)
            dve.wait_ge(scat_ps, EXPERTS + 1)
            for t in range(RT):
                for c in range(2):
                    j = V.tensor_tensor(hrow[:, t, 512 * c:512 * c + 512], bank(2 * t + c), hrow[:, t, 512 * c:512 * c + 512], ALU.add)
                j.then_inc(sum_ok, 1)
            dve.wait_ge(sq3, 1)
            V.tensor_scalar(rstat[:, 10:12], rstat[:, 8:10], 1.0 / D, EPS, ALU.mult, ALU.add).then_inc(sq3, 1)
            dve.wait_ge(sq3, 3)
            V.reciprocal(rstat[:, 12:14], rstat[:, 10:12]).then_inc(sq3, 1)
            dve.wait_ge(sq3, 4)
            dve.wait_ge(late_in, 64)
            for t in range(RT):
                V.scalar_tensor_tensor(out=final[:, t, :], in0=hrow[:, t, :], scalar=rstat[:, 12 + t:13 + t], in1=gf_bc,
                                       op0=ALU.mult, op1=ALU.mult).then_inc(out_ok, 1)


_INS = ["x", "meta_tokens", "norm1_g", "w_in", "conv_w", "conv_b", "dt_bias", "a_log", "d_skip", "ssm_norm_g",
        "w_o_attn", "w_o_ssm", "w_out", "norm2_g", "w_router", "b_router", "w_gate_up", "b_gate_up",
        "w_down", "b_down", "final_g"]


def kernel(**inputs):
    import numpy as _np
    import concourse.bacc as _bacc
    from concourse import mybir as _mybir
    from concourse.bass_utils import run_bass_kernel_spmd as _run

    nc = _bacc.Bacc("TRN2", target_bir_lowering=False, num_devices=1)
    arrays, args = {}, []
    for name in _INS:
        a = _np.ascontiguousarray(inputs[name])
        arrays[f"in_{name}_dram"] = a
        args.append(nc.dram_tensor(f"in_{name}_dram", a.shape, _mybir.dt.from_np(a.dtype), kind="ExternalInput").ap())
    args.append(nc.dram_tensor("out_dram", (1, SEQ, D), _mybir.dt.float32, kind="ExternalOutput").ap())
    build(nc, *args)
    r = _run(nc, [arrays], core_ids=[0])
    return r.results[0]["out_dram"]
```

```python
import math

import numpy as np

import concourse.bass as bass
from concourse import mybir

F32 = mybir.dt.float32
BF16 = mybir.dt.bfloat16
I32 = mybir.dt.int32
U32 = mybir.dt.uint32
ALU = mybir.AluOpType
ACT = mybir.ActivationFunctionType
AX = mybir.AxisListType

P = 128
D = 1024
SEQ = 256
N_META = 16
T_ALL = N_META + SEQ
RT = SEQ // P
KD = D // P
HEADS, HD = 16, 64
IDX_HEADS = 8
ROT = HD // 4
HALF = ROT // 2
ROPE_THETA = 500000.0
TOPK_KEYS = 64
SSM_INNER = 2 * D
SSM_HEADS = 32
GROUPS = 4
GH = SSM_HEADS // GROUPS
CONV_W = 4
CONV_TILES = (SSM_INNER + 2 * GROUPS * P) // P
EXPERTS = 32
TOP_K = 4
FF = D
LIMIT = 7.0
ALPHA = 1.702
EPS = 1e-6
SLOTS = 64
OVERFLOW_MAX = SEQ * TOP_K // SLOTS
MASKED = -3.0e38
PICKED = -3.3e38
UNROUTED = 1000.0
HELD = {27: [("gu", 0), ("gu", 1)], 28: [("gu", 0)], 29: [("gu", 0)], 30: [("gu", 0), ("dn", 3)], 31: [("gu", 0)]}
LOOPED = min(HELD)

C_Q, C_K, C_V, C_QI = 0, 1024, 2048, 3072
C_KI, C_Z, C_X, C_DT, C_GATE = 3584, 3656, 5704, 8776, 8808

BLOCKS = (["S"] + [f"X{i}" for i in range(6)] + [f"Z{i}" for i in range(4)] + ["K0", "K1", "V0", "V1", "Q0", "Q1", "QI"]
          + [f"G{i}" for i in range(4)] + [f"OS{i}" for i in range(4)] + ["OA0", "OA1", "WO0", "WO1"])
NB = {name: n for n, name in enumerate(BLOCKS)}
RING = 5
NORM_ORDER = (0, RT, 1)
K_ORDER = (1, 0) + tuple(range(2, KD))
SLOT = KD * 512


def constants():
    part = np.arange(P)[:, None]
    free = np.arange(P)[None, :]
    inv = np.exp(np.float32(-math.log(ROPE_THETA)) * np.arange(HALF, dtype=np.float32) / np.float32(HALF)).astype(np.float32)
    ang = np.arange(T_ALL, dtype=np.float32)[:, None] * inv[None, :]
    table = np.concatenate([np.cos(ang), np.sin(ang)], axis=1).astype(np.float32)
    rope = np.zeros((P, 3, ROT), np.float32)
    rope[:, 0] = table[N_META:N_META + P]
    rope[:, 1] = table[N_META + P:]
    rope[:N_META, 2] = table[:N_META]
    block = np.arange(1, 4)[:, None]
    parts = {
        "ident": (part == free),
        "tri_le": (part <= free),
        "tri_lt": (part < free),
        "ones": np.ones((P, P)),
        "slots": np.tile((SLOTS * np.arange(4)[:, None] + free % SLOTS).reshape(1, -1), (P, 1)),
        "causal": (free <= part),
        "causal_neg": np.where(free <= part, 0.0, MASKED),
        "experts": np.tile(np.arange(EXPERTS), (P, 1)),
        "row_expert": part % EXPERTS,
        "rope": rope.reshape(P, -1),
        "codes": np.tile((EXPERTS * block + np.arange(EXPERTS)[None, :]).reshape(1, -1), (P, 1)),
        "thresholds": np.tile((SLOTS * block + 0 * np.arange(EXPERTS)[None, :]).reshape(1, -1), (P, 1)),
        "turns": np.tile(np.arange(OVERFLOW_MAX), (P, 1)),
    }
    at, where = 0, {}
    for name, a in parts.items():
        where[name] = (at, at + a.shape[1])
        at += a.shape[1]
    return np.concatenate([a.astype(np.float32) for a in parts.values()], axis=1), where


def build(nc, x, meta_tokens, norm1_g, w_in, conv_w, conv_b, dt_bias, a_log, d_skip, ssm_norm_g,
          w_o_attn, w_o_ssm, w_out, norm2_g, w_router, b_router, w_gate_up, b_gate_up,
          w_down, b_down, final_g, out):
    table, where = constants()
    const_dram = nc.inline_tensor(table, name="const_table")

    def mem(name, cols, dt=F32):
        return nc.alloc_sbuf_tensor(name, [P, cols], dt)

    const = mem("const", table.shape[1])

    def cst(name):
        return const[:, where[name][0]:where[name][1]]

    ident, tri_le, tri_lt, ones = cst("ident"), cst("tri_le"), cst("tri_lt"), cst("ones")
    slots = cst("slots").rearrange("p (b s) -> p b s", b=4)
    rope_tab = cst("rope").rearrange("p (t c) -> p t c", t=3)
    weights = mem("weights", RING * SLOT)
    last_slot = mem("last_slot", SLOT)
    hrow = mem("hrow", RT * D)[:, :].rearrange("p (t d) -> p t d", t=RT)
    cols1 = mem("cols1", P)
    cols2 = mem("cols2", 24)
    small_t = mem("small", 3 * 104)
    small = small_t[:, :].rearrange("p (t c) -> p t c", t=3)
    stat = mem("stat", 64)
    hnT = mem("hnT", KD * T_ALL)[:, :].rearrange("p (k t) -> p k t", k=KD)
    ssmT = mem("ssmT", 16 * SEQ)[:, :].rearrange("p (k t) -> p k t", k=16)
    arena = mem("arena", 16800)
    bias_parts = mem("bias_parts", 2 * FF, BF16)
    conv_col = [[cols1[:, w * CONV_TILES + j:w * CONV_TILES + j + 1] for j in range(CONV_TILES)] for w in range(CONV_W)]
    convb_col = [cols1[:, 96 + j:97 + j] for j in range(CONV_TILES)]
    g1_col = [cols1[:, 120 + k:121 + k] for k in range(KD)]
    ssmg_cols = cols2[:, 0:16]
    g2_cols = cols2[:, 16:24]

    def carver(region, start=0):
        at = [start]

        def carve(n):
            at[0] += n
            assert at[0] <= region.shape[1], (at[0], region.shape)
            return region[:, at[0] - n:at[0]]
        return carve

    def split(ap, a):
        return ap.rearrange("p (a b) -> p a b", a=a)

    early = ssmT.rearrange("p k t -> p (k t)")
    xn = split(early[:, 0:3 * D], 3)
    rows1 = early[:, 3 * D:3 * D + P]
    rows2 = early[:, 3 * D + P:3 * D + 2 * P]
    bias_raw = early[0:EXPERTS, 0:2 * FF]
    bias_part16 = early[0:EXPERTS, 2 * FF:3 * FF].bitcast(BF16)
    carve = carver(arena)
    xbcT = split(carve(CONV_TILES * T_ALL), CONV_TILES)
    hmeta = carve(D)
    conv_acc = split(carve(3 * T_ALL), 3)
    bc = split(carve(3 * 32), 3)
    dt_x, dt_n, dt_e, dt_l, dtv, adt, wdec = (split(carve(96), 3) for _ in range(7))
    ea_log = carve(32)
    acs = split(carve(6 * 32), 6)
    eacs = split(carve(2 * 32), 2)
    cdec = carve(32)
    xr = split(carve(2 * 512), 2)
    xdt = split(carve(2 * 512), 2)
    xsk = split(carve(2 * 512), 2)
    br = split(carve(2 * P), 2)
    cbm = split(carve(2 * P), 2)
    ss_y = carve(16)
    argm = split(carve(2 * 512), 2)
    yrow = split(carve(2 * 512), 2)
    carve_last = carver(last_slot)
    xm = carve_last(512)
    xdec = carve_last(512)
    xmdec = carve_last(512)
    prev = split(carve_last(2 * 512), 2)
    gated = carve_last(512)
    tanh_z = carve_last(512)
    square_junk = carve_last(512)
    carve = carver(arena)
    kraw = split(carve(3 * D), 3)
    qiraw = split(carve(RT * 512), RT)
    gatesT = arena[:, 0:16 * SEQ].rearrange("p (k t) -> p k t", k=16)
    vraw = split(carve(3 * D), 3)
    qraw = split(carve(RT * D), RT)
    attnT = arena[:, 4096 + 3 * D:4096 + 5 * D].rearrange("p (k t) -> p k t", k=KD)
    qT = split(carve(KD * SEQ), KD)
    kT = split(carve(KD * T_ALL), KD)
    qiT = split(carve(4 * SEQ), 4)
    kidup = split(last_slot[:, 3552:3808], RT)
    kiT = carve(SEQ)
    amask = carve(2 * N_META + P + SEQ)
    carve_last = carver(last_slot)
    relu_b = split(carve_last(2 * 512), 2)
    score = split(carve_last(2 * SEQ), 2)
    work = split(carve_last(2 * SEQ), 2)
    ao = last_slot[:, 0:RT * D].rearrange("p (t d) -> p t d", t=RT)
    rope_tmp = split(carve_last(4 * 256), 4)
    sbuf_s = split(last_slot[:, 2048:2048 + 2 * 416], 2)
    top8 = last_slot[:, 3392:3520]
    head_stat = split(last_slot[:, 3520:3552], 4)
    pT_k = split(carve(2 * 384), 2)
    pT_m = split(last_slot[:, 2880:2880 + 512], 2)
    prob = split(carve(2 * 416), 2)
    carve = carver(arena)
    hn2 = split(carve(RT * D), RT)
    carve(2048)
    carve(3 * D)
    hn2T = split(carve(KD * SEQ), KD)
    w_r = split(carve(KD * EXPERTS), KD)
    br_bc = carve(EXPERTS)
    bdn = carve(D)
    gf_bc = carve(D)
    logit, dense_w, routed, posm = (split(carve(2 * EXPERTS), 2) for _ in range(4))
    v8, idxf, e4, w4 = (split(carve(16), 2) for _ in range(4))
    idx8 = split(mem("idx8", 16, U32)[:, :], 2)
    pick = split(carve(2 * 4 * EXPERTS), 2)
    dwT = split(carve(2 * P), 2)
    rstat = carve(16)
    count = carve(EXPERTS)
    flags, seq = carve(96), carve(96)
    n_over_f = carve(1)
    n_over = mem("n_over", 1, I32)
    codes_f = carve(OVERFLOW_MAX)
    codes = mem("codes", OVERFLOW_MAX, I32)
    xe_flat = hnT.rearrange("p k t -> p (k t)")[:, 0:512]
    xe = split(xe_flat, KD)
    actT = hnT.rearrange("p k t -> p (k t)")[:, 512:1024]
    y_sb = hnT.rearrange("p k t -> p (k t)")[:, 1024:1536]
    selT = hnT.rearrange("p k t -> p (k t)")[:, 1536:1792]
    late = ssmT.rearrange("p k t -> p (k t)")
    sel = split(late[:, 0:128], 2)
    selw = split(late[:, 128:384], 2)
    gmin, sig, upc, act = (late[:, 512 + 512 * i:1024 + 512 * i] for i in range(4))
    xrow = late[:, 2560:3072]
    one_hot = split(late[:, 2560:2560 + 96 * OVERFLOW_MAX], OVERFLOW_MAX)
    junk2 = [split(late[:, D * t:D * t + D], 2) for t in range(RT)]
    junk = [late[:, 512 * n:512 * n + 512] for n in range(4)]
    one_expert = carve(SLOTS // 2).bitcast(BF16)
    final = split(arena[:, 4096:4096 + RT * D], RT)

    end = arena.shape[1]
    free_gu = [arena[:, 4096:6144], arena[:, end - 4096:end - 2048], arena[:, end - 2048:end],
               arena[:, 2048:4096],
               arena[:, 7168:9216],
               hrow.rearrange("p t d -> p (t d)")]
    held = {}
    for e, parts in HELD.items():
        for kind, i in parts:
            held[e, kind, i] = [free_gu.pop(0)] if kind == "gu" else [arena[:, 6144:7168], late[:, 3072:4096]]
    held_gu = [key for key in held if key[1] == "gu"]
    held_dn = [key for key in held if key[1] == "dn"]

    PS = nc.alloc_psum_tensor("ps", [P, 8, 512], F32)

    def bank(i):
        return PS[:, i, :]

    def wslot(name):
        n = NB[name] % RING
        return split(weights[:, n * SLOT:(n + 1) * SLOT], KD)

    gu_chunk = [split(weights[:, 0:4 * SLOT], KD)[:, k, :] for k in range(KD)]
    dn_chunk = [weights[:, 4 * SLOT + D * k:4 * SLOT + D * (k + 1)] for k in range(4)] \
        + [last_slot[:, D * k:D * (k + 1)] for k in range(4)]

    def sem(name):
        return nc.alloc_semaphore(name)

    const_in, rows_in, vec_in, late_in = sem("const_in"), sem("rows_in"), sem("vec_in"), sem("late_in")
    x_in = [sem(f"x_in{t}") for t in range(RT + 1)]
    slot_in = [sem(f"slot_in{i}") for i in range(RING)]
    cols_ps, cols_ok = sem("cols_ps"), sem("cols_ok")
    sq1, rstd1, xn_ok, xnT_ps, hnT_ok = sem("sq1"), sem("rstd1"), sem("xn_ok"), sem("xnT_ps"), sem("hnT_ok")
    small_ps, small_ok = sem("small_ps"), sem("small_ok")
    zeroed = sem("zeroed")
    dt_dve, dt_act, acs_ps = sem("dt_dve"), sem("dt_act"), sem("acs_ps")
    conv_ps, conv_ok, xbc_ok = sem("conv_ps"), sem("conv_ok"), sem("xbc_ok")
    dve_chain, act_chain, pool_chain = sem("dve_chain"), sem("act_chain"), sem("pool_chain")
    xrow_ps, xrow_ok, bcb_ps, brow_ok, cbm_ok = sem("xrow_ps"), sem("xrow_ok"), sem("bcb_ps"), sem("brow_ok"), sem("cbm_ok")
    abc_ps, arg_ok, exp_ok, decay_ok = sem("abc_ps"), sem("arg_ok"), sem("exp_ok"), sem("decay_ok")
    pool_x = sem("pool_x")
    z_ps, tanh_ok, z_used = sem("z_ps"), sem("tanh_ok"), sem("z_used")
    state_ps, state_ok = sem("state_ps"), sem("state_ok")
    yd_ps, yo_ps, y_read = sem("yd_ps"), sem("yo_ps"), sem("y_read")
    y_ok, ysq_ok, yn_ok, yT_ps, ssmT_ok = sem("y_ok"), sem("ysq_ok"), sem("yn_ok"), sem("yT_ps"), sem("ssmT_ok")
    proj_ps, proj_ok = sem("proj_ps"), sem("proj_ok")
    kmeta_ps, kmeta_ok = sem("kmeta_ps"), sem("kmeta_ok")
    rope_ok = sem("rope_ok")
    turn_ps, turn_ok = sem("turn_ps"), sem("turn_ok")
    idx_ps, relu_ok, relu_used = sem("idx_ps"), sem("relu_ok"), sem("relu_used")
    mask_ok = sem("mask_ok")
    gate_ps, gate_ok, sigm_ok = sem("gate_ps"), sem("gate_ok"), sem("sigm_ok")
    s_ps, s_ok, prob_ok, pT_ps, pTk_ok, pTm_ok, pv_ps, ao_ok = (sem(n) for n in (
        "s_ps", "s_ok", "prob_ok", "pT_ps", "pTk_ok", "pTm_ok", "pv_ps", "ao_ok"))
    aoT_ps, attnT_ok = sem("aoT_ps"), sem("attnT_ok")
    os_ps, os_ok, oa_ps, uT_ok, wo_ps, h2_ok = (sem(n) for n in ("os_ps", "os_ok", "oa_ps", "uT_ok", "wo_ps", "h2_ok"))
    sq2, rstd2, hn2_ok, hn2T_ps = sem("sq2"), sem("rstd2"), sem("hn2_ok"), sem("hn2T_ps")
    logit_ps, negv_ok, e4_ok, dense_ok, route_ps, route_ok = (sem(n) for n in (
        "logit_ps", "negv_ok", "e4_ok", "dense_ok", "route_ps", "route_ok"))
    dwT_ok = sem("dwT_ok")
    bias_in, bias_part, gu_free, dn_free = sem("bias_in"), sem("bias_free"), sem("gu_free"), sem("dn_free")
    gu_in = [sem(f"gu_in{k}") for k in range(KD)]
    held_in = {key: sem("held_in_%d_%s%d" % key) for key in held}
    dn_in = [sem(f"dn_in{k}") for k in range(4)]
    h2T_dve, h2T_act, wr_ok, count_ok = sem("h2T_dve"), sem("h2T_act"), sem("wr_ok"), sem("count_ok")
    hot_ok, bias_ps, xrow_ps2, xrow_sb, selw_ok = (sem(n) for n in ("hot_ok", "bias_ps", "xrow_ps2", "xrow_sb", "selw_ok"))
    sel_ok, selT_ps, selT_ok, xe_ps, xe_ok, gu_ps, gmin_ok, upc_ok, upg_ok, sig_ok, act_ok = (sem(n) for n in (
        "sel_ok", "selT_ps", "selT_ok", "xe_ps", "xe_ok", "gu_ps", "gmin_ok", "upc_ok", "upg_ok", "sig_ok", "act_ok"))
    actT_ps, actT_ok, ysb_ok, scat_ps, scat_top_ps = sem("actT_ps"), sem("actT_ok"), sem("ysb_ok"), sem("scat_ps"), sem("scat_top_ps")
    codes_ok, sq3, root3, rstd3, out_ok, out_in = sem("codes_ok"), sem("sq3"), sem("root3"), sem("rstd3"), sem("out_ok"), sem("out_in")

    def block_source(name):
        if name == "S":
            w = w_in[0].rearrange("(k p) n -> p k n", p=P)
            return [(w[:, :, C_KI:C_KI + 72], 0, 72), (w[:, :, C_DT:C_DT + 32], 72, 104)]
        if name[:2] == "OS":
            c, kk = int(name[2]) // 2, int(name[2]) % 2
            w = w_o_ssm[0].rearrange("(k p) n -> p k n", p=P)
            return [(w[:, KD * kk:KD * kk + KD, 512 * c:512 * c + 512], 0, 512)]
        if name[:2] in ("OA", "WO"):
            w = (w_o_attn if name[:2] == "OA" else w_out)[0].rearrange("(k p) n -> p k n", p=P)
            c = int(name[2])
            return [(w[:, :, 512 * c:512 * c + 512], 0, 512)]
        base = {"X": C_X, "Z": C_Z, "K": C_K, "V": C_V, "Q": C_Q, "G": C_GATE}[name[0]]
        at = C_QI if name == "QI" else base + 512 * int(name[1])
        return [(w_in[0].rearrange("(k p) n -> p k n", p=P)[:, :, at:at + 512], 0, 512)]

    def loaded(eng, name):
        n = NB[name]
        uses = sum(2 if BLOCKS[m] == "S" else 1 for m in range(n % RING, n + 1, RING))
        eng.wait_ge(slot_in[n % RING], 16 * uses)

    def used_up(name):
        i = int(name[-1]) if name[-1].isdigit() else 0
        return {"S": (small_ps, 1), "X": (conv_ps, 4 * i + 4), "Z": (z_ps, 2 * i + 2), "K": (kmeta_ps, 1), "V": (kmeta_ps, 1),
                "Q": (proj_ps, 14 if name == "QI" else 10 + 2 * i), "G": (gate_ps, 4 * i + 4), "OS": (os_ps, 4 * (i // 2) + 4),
                "OA": (oa_ps, 4 * i + 4), "WO": (wo_ps, i + 3)}[name if name == "S" else name[:-1]]

    def real(t):
        return slice(N_META + P * t, N_META + P * t + P)

    block = nc.Block()
    with block:
        @block.sync
        def _(sp):
            for t in NORM_ORDER:
                if t < RT:
                    sp.dma_start(hrow[:, t, :], x[0, P * t:P * t + P, :]).then_inc(x_in[t], 16)
                else:
                    sp.dma_start(hmeta[0:N_META, :], meta_tokens).then_inc(x_in[t], 16)
            sp.dma_start(rows1[96:120, :], conv_b[0].rearrange("(j p) -> j p", p=P)).then_inc(rows_in, 16)
            sp.dma_start(rows1[120:128, :], norm1_g[0].rearrange("(j p) -> j p", p=P)).then_inc(rows_in, 16)
            sp.dma_start(rows2[0:16, :], ssm_norm_g[0].rearrange("(j p) -> j p", p=P)).then_inc(rows_in, 16)
            sp.dma_start(rows2[16:24, :], norm2_g[0].rearrange("(j p) -> j p", p=P)).then_inc(rows_in, 16)
            for i, v in enumerate((dt_bias, a_log, d_skip)):
                sp.dma_start(bc[:, i, :], v[0].partition_broadcast(P)).then_inc(vec_in, 16)

            def load_held(keys):
                for e, kind, i in keys:
                    for part, rows in zip(held[e, kind, i], (2 * i, 2 * i + 1) if kind == "dn" else (i,)):
                        w = w_down if kind == "dn" else w_gate_up
                        sp.dma_start(part, w[0, e, P * rows:P * rows + P, :]).then_inc(held_in[e, kind, i], 16)

            def load_down(e, i):
                src = w_down[0, bass.ds(e, 1), 2 * i * P:(2 * i + 2) * P, :].rearrange("e (k p) n -> p (e k) n", p=P)
                region = weights[:, 4 * SLOT + 2 * D * i:4 * SLOT + 2 * D * (i + 1)] if i < 2 \
                    else last_slot[:, 2 * D * (i - 2):2 * D * (i - 1)]
                sp.dma_start(split(region, 2), src).then_inc(dn_in[i], 16)

            def load_gate_up(e, k):
                sp.dma_start(gu_chunk[k], w_gate_up[0, bass.ds(e, 1), k * P:(k + 1) * P, :].rearrange("e p n -> (e p) n")).then_inc(gu_in[k], 16)

            for n, name in enumerate(BLOCKS):
                if name == "X0":
                    sp.wait_ge(rows_in, 80)
                if name == "OA1":
                    sp.wait_ge(ao_ok, HEADS)
                    sp.dma_start(w_r, w_router[0].rearrange("(k p) n -> p k n", p=P)).then_inc(late_in, 16)
                    sp.dma_start(br_bc, b_router[0].partition_broadcast(P)).then_inc(late_in, 16)
                    sp.dma_start(bdn[0:EXPERTS, :], b_down[0]).then_inc(late_in, 16)
                    sp.dma_start(gf_bc, final_g.partition_broadcast(P)).then_inc(late_in, 16)
                    load_held(held_gu[0:3])
                    load_down(0, 3)
                if n >= RING:
                    sp.wait_ge(*used_up(BLOCKS[n - RING]))
                if name == "X4":
                    sp.wait_ge(hnT_ok, KD)
                    sp.dma_start(bias_raw, b_gate_up[0]).then_inc(bias_in, 16)
                for src, a, b in block_source(name):
                    sp.dma_start(wslot(name)[:, :, a:b], src).then_inc(slot_in[n % RING], 16)

            def load_expert(u, e, peeled=False):
                def place_free(freed, parts, key):
                    ago = 1
                    while peeled and key in HELD.get(u - ago, []):
                        ago += 1
                    sp.wait_ge(freed, (u - ago) * parts + 1 + key[1])

                for k in range(KD):
                    if peeled and ("gu", k) in HELD.get(u, []):
                        continue
                    place_free(gu_free, KD, ("gu", k))
                    load_gate_up(e, k)
                for i in range(4):
                    if not (peeled and ("dn", i) in HELD.get(u, [])):
                        place_free(dn_free, 4, ("dn", i))
                        load_down(e, i)

            sp.wait_ge(aoT_ps, KD)
            load_down(0, 2)
            load_held(held_dn)
            for k in range(KD):
                if k == 6:
                    sp.wait_ge(uT_ok, KD)
                    load_held(held_gu[3:4])
                sp.wait_ge(*used_up(("OS3", "OA0", "OA1", "WO0")[k // 2]))
                load_gate_up(0, k)
            sp.wait_ge(*used_up("WO1"))
            load_down(0, 0)
            load_down(0, 1)
            sp.wait_ge(logit_ps, 2)
            load_held(held_gu[4:5])
            sp.wait_ge(hn2_ok, RT)
            sp.wait_ge(scat_ps, 1)
            load_held(held_gu[5:])
            with sp.Fori(1, LOOPED) as u:
                load_expert(u, u)
            for u in range(LOOPED, EXPERTS):
                load_expert(u, u, peeled=True)
            sp.wait_ge(route_ok, 1)
            over = sp.value_load(n_over[0:1, 0:1], min_val=0, max_val=OVERFLOW_MAX)
            with sp.If(over > 0):
                sp.wait_ge(codes_ok, 1)
                with sp.Fori(0, over) as j:
                    jj = nc.s_assert_within(j, 0, OVERFLOW_MAX - 1)
                    code = sp.value_load(codes[0:1, bass.ds(jj, 1)], min_val=0, max_val=4 * EXPERTS - 1)
                    load_expert(jj + EXPERTS, code % EXPERTS)
            for t in range(RT):
                sp.wait_ge(out_ok, t + 1)
                sp.dma_start(out[0, P * t:P * t + P, :], final[:, t, :]).then_inc(out_in, 16)
            sp.wait_ge(out_in, 16 * RT)

        @block.gpsimd
        def _(pool):
            def per_head(v):
                return v.unsqueeze(2).broadcast_to([v.shape[0], GH, HD])

            pool.wait_ge(bias_in, 16)
            for i in range(3):
                pool.tensor_copy(bias_part16, bias_raw).then_inc(bias_part, 1)
                pool.wait_ge(bias_part, 2 * i + 1)
                pool.tensor_copy(bias_parts[EXPERTS * i:EXPERTS * i + EXPERTS, :], bias_part16)
                pool.tensor_tensor(bias_raw, bias_raw, bias_part16, ALU.subtract).then_inc(bias_part, 1)
                pool.wait_ge(bias_part, 2 * i + 2)
            pool.wait_ge(vec_in, 48)
            pool.wait_ge(dt_dve, 5)
            for g in range(GROUPS):
                hs = slice(GH * g, GH * g + GH)
                for t in range(RT):
                    pool.wait_ge(xrow_ok, 3 * g + t + 1)
                    if g:
                        pool.wait_ge(yd_ps, 2 * g)
                        pool.wait_ge(y_ok, 2 * g)
                    pool.tensor_tensor(xdt[:, t].rearrange("p (h e) -> p h e", h=GH), xr[:, t].rearrange("p (h e) -> p h e", h=GH),
                                       per_head(dtv[:, t, hs]), ALU.mult).then_inc(pool_x, 1)
                    pool.tensor_tensor(xsk[:, t].rearrange("p (h e) -> p h e", h=GH), xr[:, t].rearrange("p (h e) -> p h e", h=GH),
                                       per_head(bc[:, 2, hs]), ALU.mult).then_inc(pool_x, 1)
                    if t == 0:
                        if g:
                            pool.wait_ge(state_ps, 2 * g)
                        pool.tensor_tensor(xdec.rearrange("p (h e) -> p h e", h=GH), xr[:, t].rearrange("p (h e) -> p h e", h=GH),
                                           per_head(wdec[:, 0, hs]), ALU.mult).then_inc(pool_x, 1)
                pool.wait_ge(xrow_ok, 3 * g + 3)
                pool.tensor_tensor(xmdec[0:N_META].rearrange("p (h e) -> p h e", h=GH), xm[0:N_META].rearrange("p (h e) -> p h e", h=GH),
                                   per_head(wdec[0:N_META, 2, hs]), ALU.mult).then_inc(pool_x, 1)

        @block.tensor
        def _(pe):
            def turn(dst, src):
                return pe.transpose(dst, src, ident[0:src.shape[0], 0:src.shape[0]])

            pe.wait_ge(const_in, 16)
            pe.wait_ge(rows_in, 80)
            turn(bank(0)[:, 0:P], rows1)
            turn(bank(0)[:, P:P + 24], rows2[0:24, :]).then_inc(cols_ps, 1)
            pe.wait_ge(cols_ok, 1)
            for i, t in enumerate(NORM_ORDER):
                pe.wait_ge(xn_ok, i + 1)
                for k in K_ORDER:
                    mm = turn(bank(k)[:, real(t) if t < RT else slice(0, N_META)], xn[0:P if t < RT else N_META, t, P * k:P * k + P])
                    if i == len(NORM_ORDER) - 1:
                        mm.then_inc(xnT_ps, 1)

            def small_proj():
                loaded(pe, "S")
                for t in range(3):
                    rows = real(t) if t < 2 else slice(0, N_META)
                    m = P if t < 2 else N_META
                    for k in range(KD):
                        mm = pe.matmul(bank(0)[0:m, 104 * t:104 * t + 104], hnT[:, k, rows], wslot("S")[:, k, 0:104],
                                       start=(k == 0), stop=(k == KD - 1))
                mm.then_inc(small_ps, 1)

            for j in range(CONV_TILES):
                name = f"X{j // 4}"
                if j % 4 == 0:
                    loaded(pe, name)
                if j >= 7:
                    pe.wait_ge(conv_ok, j - 6)
                for i, k in enumerate(K_ORDER):
                    if j == 0:
                        pe.wait_ge(hnT_ok, i + 1)
                    mm = pe.matmul(bank(1 + j % 7)[:, 0:T_ALL], wslot(name)[:, k, P * (j % 4):P * (j % 4) + P], hnT[:, k, :],
                                   start=(i == 0), stop=(i == KD - 1))
                mm.then_inc(conv_ps, 1)
                if j == 0:
                    small_proj()
                if j == 9:
                    pe.wait_ge(dt_dve, 3)
                    pe.wait_ge(small_ok, 1)
                    for t in range(3):
                        n = P if t < 2 else N_META
                        pe.matmul(bank(0)[:, 32 * t:32 * t + 32], tri_le[0:n, :], adt[0:n, t, :], start=True, stop=True)
                        mm = pe.matmul(bank(0)[:, 96 + 32 * t:128 + 32 * t], ones[0:n, :], adt[0:n, t, :], start=True, stop=True)
                    mm.then_inc(acs_ps, 1)

            def abc(g, t, hf):
                n = 4 * g + 2 * t + hf
                if n >= 2:
                    pe.wait_ge(arg_ok, n - 1)
                for q in range(4):
                    h = GH * g + 4 * hf + q
                    mm = pe.matmul(bank(4 + hf)[:, P * q:P * q + P], adt[:, t, h:h + 1].broadcast_to([P, P]), tri_le,
                                   start=True, stop=True)
                mm.then_inc(abc_ps, 1)

            def z_proj(g, t):
                if g or t:
                    pe.wait_ge(z_used, 2 * g + t)
                for k in range(KD):
                    mm = pe.matmul(bank(7), hnT[:, k, real(t)], wslot(f"Z{g}")[:, k, :], start=(k == 0), stop=(k == KD - 1))
                mm.then_inc(z_ps, 1)

            def y_diag(g, t):
                pe.wait_ge(decay_ok, 4 * g + 2 * t + 2)
                pe.wait_ge(pool_x, 6 * g + (1 if t == 0 else 4))
                if g or t:
                    pe.wait_ge(y_read, 2 * g + t)
                for q in range(GH):
                    mm = pe.matmul(bank(6)[:, HD * q:HD * q + HD], argm[:, q // 4, P * (q % 4):P * (q % 4) + P],
                                   xdt[:, t, HD * q:HD * q + HD], start=True, stop=True)
                mm.then_inc(yd_ps, 1)

            def y_turn(g):
                for t in range(RT):
                    pe.wait_ge(yn_ok, 2 * g + t + 1)
                    for j in range(4):
                        mm = turn(bank(t)[:, P * j:P * j + P], yrow[:, t, P * j:P * j + P])
                    mm.then_inc(yT_ps, 1)

            pe.wait_ge(xbc_ok, 4)
            pe.wait_ge(dt_act, 2)
            pe.wait_ge(conv_ok, CONV_TILES - 1)
            for g in range(GROUPS):
                abc(g, 0, 0)
                abc(g, 0, 1)
                if g:
                    pe.wait_ge(y_read, 2 * g)
                for t in range(RT):
                    for j in range(4):
                        mm = turn(bank(t)[:, P * j:P * j + P], xbcT[:, 4 * g + j, real(t)])
                    mm.then_inc(xrow_ps, 1)
                if g:
                    pe.wait_ge(state_ok, 2 * g)
                for j in range(4):
                    mm = turn(bank(2)[0:N_META, P * j:P * j + P], xbcT[:, 4 * g + j, 0:N_META])
                mm.then_inc(xrow_ps, 1)
                pe.wait_ge(*((cbm_ok, g) if g else (xbc_ok, CONV_TILES)))
                turn(bank(3)[:, 0:P], xbcT[:, 16 + g, real(0)])
                turn(bank(3)[0:N_META, P:2 * P], xbcT[:, 16 + g, 0:N_META])
                for t in range(RT):
                    mm = pe.matmul(bank(3)[:, 256 + P * t:384 + P * t], xbcT[:, 16 + g, real(t)], xbcT[:, 20 + g, real(t)],
                                   start=True, stop=True)
                mm.then_inc(bcb_ps, 1)
                loaded(pe, f"Z{g}")
                z_proj(g, 0)
                if g:
                    pe.wait_ge(xrow_ok, 3 * g + 3)
                    y_turn(g - 1)
                pe.wait_ge(xrow_ok, 3 * g + 3)
                pe.wait_ge(brow_ok, g + 1)
                pe.wait_ge(pool_x, 6 * g + 6)
                pe.matmul(bank(2), br[0:N_META, 1, :], xmdec[0:N_META, :], start=True, stop=True).then_inc(state_ps, 1)
                y_diag(g, 0)
                abc(g, 1, 0)
                abc(g, 1, 1)
                pe.wait_ge(state_ok, 2 * g + 1)
                if g:
                    pe.wait_ge(ssmT_ok, 2 * g)
                pe.matmul(bank(0), xbcT[:, 20 + g, real(0)], prev[:, 0, :], start=True, stop=True).then_inc(yo_ps, 1)
                pe.matmul(bank(2), br[:, 0, :], xdec, start=True, stop=True).then_inc(state_ps, 1)
                z_proj(g, 1)
                y_diag(g, 1)
                pe.wait_ge(state_ok, 2 * g + 2)
                pe.matmul(bank(1), xbcT[:, 20 + g, real(1)], prev[:, 1, :], start=True, stop=True).then_inc(yo_ps, 1)

            step = [0]

            def rows_proj(name, t):
                n = step[0]
                step[0] += 1
                loaded(pe, name)
                if n == 0:
                    pe.wait_ge(y_read, 2 * GROUPS)
                    pe.wait_ge(z_used, 2 * GROUPS)
                    pe.wait_ge(state_ok, 2 * GROUPS)
                if n >= 6:
                    pe.wait_ge(proj_ok, n - 5)
                for k in range(KD):
                    mm = pe.matmul(bank(2 + n % 6), hnT[:, k, real(t)], wslot(name)[:, k, :], start=(k == 0), stop=(k == KD - 1))
                mm.then_inc(proj_ps, 1)

            for name in ("K0", "K1"):
                for t in range(RT):
                    rows_proj(name, t)
                if name == "K0":
                    y_turn(GROUPS - 1)
            for name in ("V0", "V1"):
                for t in range(RT):
                    rows_proj(name, t)
            pe.wait_ge(ssmT_ok, 2 * GROUPS)
            for k in range(KD):
                for i, name in enumerate(("K0", "K1", "V0", "V1")):
                    mm = pe.matmul(bank(0)[32 * i:32 * i + N_META, :], hnT[:, k, 0:N_META], wslot(name)[:, k, :],
                                   start=(k == 0), stop=(k == KD - 1))
            mm.then_inc(kmeta_ps, 1)
            for name in ("Q0", "Q1", "QI"):
                for t in range(RT):
                    rows_proj(name, t)

            pe.wait_ge(kmeta_ok, 1)
            pe.wait_ge(proj_ok, 14)
            m = 0

            def turned(parts):
                nonlocal m
                if m >= 8:
                    pe.wait_ge(turn_ok, m - 7)
                for dst, src in parts:
                    mm = turn(bank(m % 8)[:, dst], src)
                mm.then_inc(turn_ps, 1)
                m += 1

            pe.wait_ge(rope_ok, 2)
            for k in range(KD):
                turned([(slice(0, N_META), kraw[0:N_META, 2, P * k:P * k + P]), (real(0), kraw[:, 0, P * k:P * k + P]),
                        (real(1), kraw[:, 1, P * k:P * k + P])])
            pe.wait_ge(rope_ok, 5)
            turned([(slice(P * t, P * t + P), kidup[:, t, :]) for t in range(RT)])
            for k in range(4):
                turned([(slice(P * t, P * t + P), qiraw[:, t, P * k:P * k + P]) for t in range(RT)])
            for k in range(KD):
                turned([(slice(P * t, P * t + P), qraw[:, t, P * k:P * k + P]) for t in range(RT)])
            pe.wait_ge(turn_ok, m)
            n = 0
            for t in range(RT):
                keys = P * (t + 1)
                for i in range(4):
                    if n >= 3:
                        pe.wait_ge(relu_ok, n - 2)
                    for o in range(2):
                        mm = pe.matmul(bank(2 * (n % 3) + o)[:, 0:keys], qiT[64 * o:64 * o + 64, i, P * t:P * t + P],
                                       kiT[64 * o:64 * o + 64, 0:keys], start=True, stop=True)
                    mm.then_inc(idx_ps, 1)
                    n += 1

            def gate(m):
                name = f"G{m // 4}"
                loaded(pe, name)
                if m >= 2:
                    pe.wait_ge(gate_ok, m - 1)
                for k in range(KD):
                    mm = pe.matmul(bank(6 + m % 2)[:, 0:SEQ], wslot(name)[:, k, P * (m % 4):P * (m % 4) + P], hnT[:, k, N_META:T_ALL],
                                   start=(k == 0), stop=(k == KD - 1))
                mm.then_inc(gate_ps, 1)

            def scores(h):
                if h >= 2:
                    pe.wait_ge(s_ok, h - 1)
                o, k = 64 * (h % 2), h // 2
                pe.matmul(bank(h % 2)[:, 0:N_META + P], qT[o:o + 64, k, 0:P], kT[o:o + 64, k, 0:N_META + P], start=True, stop=True)
                pe.matmul(bank(h % 2)[:, N_META + P:416], qT[o:o + 64, k, P:SEQ], kT[o:o + 64, k, :],
                          start=True, stop=True).then_inc(s_ps, 1)

            def turn_probs(h):
                pe.wait_ge(prob_ok, h + 1)
                if h >= 1:
                    pe.wait_ge(pTm_ok, h)
                if h >= 2:
                    pe.wait_ge(pTk_ok, h - 1)
                p = prob[:, h % 2]
                turn(bank(4)[0:N_META, 0:P], p[:, 0:N_META])
                turn(bank(4)[0:N_META, P:2 * P], p[:, 144:160])
                for i, at in enumerate((16, 160, 288)):
                    mm = turn(bank(2 + h % 2)[:, P * i:P * i + P], p[:, at:at + P])
                mm.then_inc(pT_ps, 1)

            def values(h):
                pe.wait_ge(pTk_ok, h + 1)
                pe.wait_ge(pTm_ok, h + 1)
                if h >= 1:
                    pe.wait_ge(ao_ok, h)
                pk, pm, hc = pT_k[:, h % 2], pT_m[:, h % 2], slice(HD * h, HD * h + HD)
                for t in range(RT):
                    o = bank(5)[:, P * (h % 2) + HD * t:P * (h % 2) + HD * t + HD]
                    pe.matmul(o, pm[0:N_META, P * t:P * t + P], vraw[0:N_META, 2, hc], start=True, stop=False)
                    for s in range(t + 1):
                        i = t + s
                        mm = pe.matmul(o, pk[:, P * i:P * i + P], vraw[:, s, hc], start=False, stop=(s == t))
                mm.then_inc(pv_ps, 1)

            for m in range(3):
                gate(m)
            pe.wait_ge(mask_ok, 1)
            scores(0)
            for h in range(HEADS):
                if h + 1 < HEADS:
                    scores(h + 1)
                if h + 3 < 16:
                    gate(h + 3)
                if h:
                    values(h - 1)
                turn_probs(h)
            values(HEADS - 1)

            def o_proj(parts, rhs, m, ps, done):
                for i, (name, k, r) in enumerate(parts):
                    if k == 0:
                        loaded(pe, name)
                    mm = pe.matmul(bank(ps)[:, 0:SEQ], wslot(name)[:, k, P * (m % 4):P * (m % 4) + P], rhs[:, r, :],
                                   start=(i == 0), stop=(i == len(parts) - 1))
                mm.then_inc(done, 1)

            pe.wait_ge(gate_ok, 16)
            for m in range(8):
                if m >= 2:
                    pe.wait_ge(os_ok, m - 1)
                o_proj([(f"OS{2 * (m // 4) + kk}", k, KD * kk + k) for kk in range(2) for k in range(KD)], ssmT, m, 6 + m % 2, os_ps)
            pe.wait_ge(ao_ok, HEADS)
            for k in range(KD):
                if k >= 4:
                    pe.wait_ge(attnT_ok, k - 3)
                for t in range(RT):
                    mm = turn(bank(k % 4)[:, P * t:P * t + P], ao[:, t, P * k:P * k + P])
                mm.then_inc(aoT_ps, 1)
            pe.wait_ge(attnT_ok, KD)
            for m in range(8):
                if m >= 2:
                    pe.wait_ge(uT_ok, m - 1)
                o_proj([(f"OA{m // 4}", k, k) for k in range(KD)], attnT, m, 4 + m % 2, oa_ps)
            pe.wait_ge(uT_ok, 8)
            def out_proj(t, c):
                loaded(pe, f"WO{c}")
                for k in range(KD):
                    mm = pe.matmul(bank(2 * t + c), gatesT[:, k, P * t:P * t + P], wslot(f"WO{c}")[:, k, :],
                                   start=(k == 0), stop=(k == KD - 1))
                mm.then_inc(wo_ps, 1)

            def turn_rows(t):
                pe.wait_ge(h2_ok, 2 * t + 2)
                for k in range(KD):
                    mm = turn(bank(4 + 2 * t + k // 4)[:, P * (k % 4):P * (k % 4) + P], hrow[:, t, P * k:P * k + P])
                mm.then_inc(hn2T_ps, 1)

            def router(t):
                pe.wait_ge(h2T_dve, t + 1)
                pe.wait_ge(h2T_act, t + 1)
                for k in range(KD):
                    mm = pe.matmul(bank(4 + 2 * t)[:, 0:EXPERTS], hn2T[:, k, P * t:P * t + P], w_r[:, k, :],
                                   start=(k == 0), stop=(k == KD - 1))
                mm.then_inc(logit_ps, 1)

            out_proj(0, 0)
            out_proj(0, 1)
            out_proj(1, 0)
            turn_rows(0)
            out_proj(1, 1)
            pe.wait_ge(wr_ok, 1)
            router(0)
            turn_rows(1)
            router(1)

            def open_sums(t):
                for c in range(2):
                    mm = pe.matmul(bank(2 * t + c), ident, hrow[:, t, 512 * c:512 * c + 512], start=True, stop=False, skip_group_check=True)
                return mm

            open_sums(0)
            pe.wait_ge(dense_ok, 1)
            pe.matmul(bank(6)[:, 0:32], tri_lt, routed[:, 0, :], start=True, stop=True)
            pe.matmul(bank(6)[:, 32:64], ones, routed[:, 0, :], start=True, stop=False)
            pe.matmul(bank(6)[:, 32:64], tri_lt, routed[:, 1, :], start=False, stop=True).then_inc(route_ps, 1)
            for t in range(RT):
                mm = pe.matmul(bank(4)[:, 0:32], ones, routed[:, t, :], start=(t == 0), stop=(t == 1))
            for t in range(RT):
                mm = turn(bank(7)[0:EXPERTS, P * t:P * t + P], dense_w[:, t, :])
            mm.then_inc(route_ps, 1)
            open_sums(1).then_inc(scat_ps, 1)

            def down_bias(quarters):
                for n in quarters:
                    t, c = n // 2, n % 2
                    pe.matmul(bank(n), dwT[0:EXPERTS, t, :], bdn[0:EXPERTS, 512 * c:512 * c + 512],
                              start=False, stop=False, skip_group_check=True)

            quarters = [(b, a) for b in range(2) for a in range(2)]

            def gather(u):
                pe.wait_ge(hn2_ok, 2)
                pe.wait_ge(sel_ok, u + 1)
                for t in range(RT):
                    for c in range(2):
                        mm = pe.matmul(bank(6)[64 * c:64 * c + 64, :], sel[:, t, :], hn2[:, t, 512 * c:512 * c + 512],
                                       start=(t == 0), stop=(t == RT - 1))
                mm.then_inc(xrow_ps2, 1)

            def turn_tokens(u):
                pe.wait_ge(xrow_sb, u + 1)
                for j in range(4):
                    mm = turn(bank(5)[:, P * j:P * j + P], xrow[:, P * j:P * j + P])
                mm.then_inc(xe_ps, 1)

            def start_bias(u):
                pe.wait_ge(xe_ok, u + 1)
                pe.wait_ge(hot_ok, u + 1)
                for b, a in quarters:
                    mm = pe.matmul(bank(4 + b)[64 * a:64 * a + 64, :], one_expert[0:96, :],
                                   bias_parts[0:96, FF * b + 512 * a:FF * b + 512 * a + 512], start=True, stop=False)
                mm.then_inc(bias_ps, 1)

            def part_of(u, kind, i, peeled):
                if isinstance(u, int) and (u, kind, i) in held:
                    parts = held[u, kind, i]
                    pe.wait_ge(held_in[u, kind, i], 16 * len(parts))
                    return parts
                skipped = sum((kind, i) in parts for parts in HELD.values()) if not isinstance(u, int) and peeled else \
                    sum((kind, i) in parts for e, parts in HELD.items() if e < u) if peeled else 0
                pe.wait_ge((gu_in if kind == "gu" else dn_in)[i], (u - skipped) * 16 + 16)
                return None

            def gate_up(u, peeled):
                for k in range(KD):
                    w = part_of(u, "gu", k, peeled)
                    w = w[0] if w else gu_chunk[k]
                    for b, a in quarters:
                        mm = pe.matmul(bank(4 + b)[64 * a:64 * a + 64, :], xe[:, 2 * (k % 4) + k // 4, :],
                                       w[:, FF * b + 512 * a:FF * b + 512 * a + 512], start=False, stop=(k == KD - 1))
                    mm.then_inc(gu_free, 1)

            def turn_selection(u):
                pe.wait_ge(selw_ok, u + 1)
                for t in range(RT):
                    mm = turn(bank(7)[:, P * t:P * t + P], selw[:, t, :])
                mm.then_inc(selT_ps, 1)

            def turn_act(u):
                pe.wait_ge(act_ok, u + 1)
                for j in range(4):
                    mm = turn(bank(4)[:, P * j:P * j + P], act[:, P * j:P * j + P])
                mm.then_inc(actT_ps, 1)

            def down(u, peeled):
                pe.wait_ge(actT_ok, u + 1)
                pe.wait_ge(selT_ok, u + 1)
                for kk in range(KD):
                    a, j = kk // 4, kk % 4
                    if kk % 2 == 0:
                        pair = part_of(u, "dn", kk // 2, peeled) or dn_chunk[kk:kk + 2]
                    for c in range(2):
                        mm = pe.matmul(bank(7)[64 * c:64 * c + 64, :], actT[:, P * j + SLOTS * a:P * j + SLOTS * a + SLOTS],
                                       pair[kk % 2][:, 512 * c:512 * c + 512], start=(kk == 0), stop=(kk == KD - 1))
                    if kk % 2:
                        mm.then_inc(dn_free, 1)

            def scatter(u):
                pe.wait_ge(ysb_ok, u + 1)
                for t in range(RT):
                    for c in range(2):
                        mm = pe.matmul(bank(2 * t + c), selT[64 * c:64 * c + 64, P * t:P * t + P], y_sb[64 * c:64 * c + 64, :],
                                       start=False, stop=False, skip_group_check=True)
                    mm.then_inc(scat_ps if t else scat_top_ps, 1)

            def prepare(u):
                gather(u)
                turn_tokens(u)
                start_bias(u)

            def unit(u, ahead, peeled=False):
                gate_up(u, peeled)
                turn_selection(u)
                if ahead:
                    gather(u + 1)
                elif isinstance(u, int):
                    down_bias(range(3))
                turn_act(u)
                if ahead:
                    turn_tokens(u + 1)
                elif isinstance(u, int):
                    down_bias(range(3, 4))
                down(u, peeled)
                if ahead:
                    start_bias(u + 1)
                scatter(u)

            pe.wait_ge(bias_part, 6)
            pe.wait_ge(count_ok, 1)
            pe.wait_ge(dwT_ok, 1)
            prepare(0)
            with pe.Fori(0, LOOPED) as u:
                unit(u, True)
            for u in range(LOOPED, EXPERTS):
                unit(u, u < EXPERTS - 1, peeled=True)
            over = pe.value_load(n_over[0:1, 0:1], min_val=0, max_val=OVERFLOW_MAX)
            with pe.If(over > 0):
                with pe.Fori(0, over) as j:
                    prepare(j + EXPERTS)
                    unit(j + EXPERTS, False, peeled=True)

        @block.scalar
        def _(act_e):
            chain = [0]

            def link(ins):
                chain[0] += 1
                ins.then_inc(act_chain, 1)
                act_e.wait_ge(act_chain, chain[0])

            def act_f(o, i, f, **kw):
                return nc.scalar.activation(o, i, f, **kw)

            def copy(o, i):
                return nc.scalar.activation(o, i, ACT.Copy)

            act_e.dma_start(const[:, :], const_dram[:, :]).then_inc(const_in, 16)
            act_e.dma_start(rows1[0:96, :], conv_w[0].rearrange("w (j p) -> (w j) p", p=P)).then_inc(rows_in, 16)
            act_e.wait_ge(zeroed, 2)
            act_f(stat[:, 9:10], stat[:, 8:9], ACT.Sqrt)
            for i, t in enumerate(NORM_ORDER):
                n = P if t < RT else N_META
                src = hrow[:, t, :] if t < RT else hmeta[0:n, :]
                act_e.wait_ge(x_in[t], 16)
                act_f(xn[0:n, t, :], src, ACT.Square, accum_out=stat[0:n, t:t + 1]).then_inc(sq1, 1)
                act_e.wait_ge(sq1, i + 1)
                act_f(stat[0:n, 3 + t:4 + t], stat[0:n, t:t + 1], ACT.Sqrt, scale=1.0 / D, bias=stat[0:n, 8:9]).then_inc(rstd1, 1)
            act_e.wait_ge(small_ps, 1)
            copy(small[:, 0:2, :].rearrange("p t c -> p (t c)"), bank(0)[:, 0:208])
            copy(small[0:N_META, 2, :], bank(0)[0:N_META, 208:312]).then_inc(small_ok, 1)
            act_e.wait_ge(dt_dve, 1)
            link(act_f(dt_e, dt_n, ACT.Exp))
            act_e.wait_ge(vec_in, 48)
            act_f(ea_log, bc[:, 1, :], ACT.Exp)
            act_f(dt_l, dt_e, ACT.Ln, bias=ones[:, 0:1]).then_inc(dt_act, 1)

            for j in range(CONV_TILES):
                act_e.wait_ge(conv_ok, j + 1)
                act_f(xbcT[:, j, :], conv_acc[:, j % 3, :], ACT.Silu, bias=convb_col[j]).then_inc(xbc_ok, 1)
                if j == 11:
                    act_e.wait_ge(acs_ps, 1)
                    copy(acs.rearrange("p a b -> p (a b)"), bank(0)[:, 0:192]).then_inc(dt_act, 1)
            act_e.wait_ge(dt_dve, 4)
            act_e.wait_ge(dt_act, 2)
            act_f(eacs, acs[:, 0:2, :], ACT.Exp)
            act_f(cdec, acs[:, 3, :], ACT.Exp)
            act_f(wdec, wdec, ACT.Exp).then_inc(dt_act, 1)

            def y_square(g, t):
                act_e.wait_ge(y_ok, 2 * g + t + 1)
                link(act_f(square_junk, yrow[:, t, :], ACT.Square, accum_out=ss_y[:, 2 * (g % 4) + t:2 * (g % 4) + t + 1]))
                act_e.wait_ge(act_chain, chain[0])
                act_f(ss_y[:, 8 + 2 * g + t:9 + 2 * g + t], ss_y[:, 2 * g + t:2 * g + t + 1], ACT.Sqrt,
                      scale=1.0 / 512, bias=stat[:, 8:9]).then_inc(ysq_ok, 1)

            for g in range(GROUPS):
                for t in range(RT):
                    act_e.wait_ge(xrow_ps, 3 * g + t + 1)
                    if g:
                        act_e.wait_ge(pool_x, 6 * g)
                    copy(xr[:, t, :], bank(t)).then_inc(xrow_ok, 1)
                act_e.wait_ge(xrow_ps, 3 * g + 3)
                copy(xm[0:N_META, :], bank(2)[0:N_META, :]).then_inc(xrow_ok, 1)
                act_e.wait_ge(bcb_ps, g + 1)
                copy(br[:, 0, :], bank(3)[:, 0:P])
                copy(br[0:N_META, 1, :], bank(3)[0:N_META, P:2 * P]).then_inc(brow_ok, 1)
                for t in range(RT):
                    for hf in range(2):
                        act_e.wait_ge(arg_ok, 4 * g + 2 * t + hf + 1)
                        act_f(argm[:, hf, :], argm[:, hf, :], ACT.Exp).then_inc(exp_ok, 1)
                    if t == 0:
                        act_e.wait_ge(state_ps, 2 * g + 1)
                        copy(prev[:, 0, :], bank(2)).then_inc(state_ok, 1)
                    act_e.wait_ge(z_ps, 2 * g + t + 1)
                    act_f(tanh_z, bank(7), ACT.Tanh, scale=0.5).then_inc(tanh_ok, 1)
                    if t:
                        for tt in range(RT):
                            y_square(g, tt)

            dst = [kraw[:, t, 512 * c:512 * c + 512] for c in range(2) for t in range(RT)] \
                + [vraw[:, t, 512 * c:512 * c + 512] for c in range(2) for t in range(RT)]
            for n, d in enumerate(dst):
                act_e.wait_ge(proj_ps, n + 1)
                if n == 0:
                    act_e.wait_ge(ssmT_ok, 2 * GROUPS)
                copy(d, bank(2 + n % 6)).then_inc(proj_ok, 1)
            act_e.wait_ge(kmeta_ps, 1)
            copy(kraw[0:N_META, 2, 0:512], bank(0)[0:N_META, :])
            copy(kraw[0:N_META, 2, 512:D], bank(0)[32:32 + N_META, :])
            copy(vraw[0:N_META, 2, 0:512], bank(0)[64:64 + N_META, :])
            copy(vraw[0:N_META, 2, 512:D], bank(0)[96:96 + N_META, :]).then_inc(kmeta_ok, 1)
            dst = [qraw[:, t, 512 * c:512 * c + 512] for c in range(2) for t in range(RT)] + [qiraw[:, t, :] for t in range(RT)]
            for n, d in enumerate(dst):
                act_e.wait_ge(proj_ps, 8 + n + 1)
                copy(d, bank(2 + (8 + n) % 6)).then_inc(proj_ok, 1)
            dst = [kT[:, k, :] for k in range(KD)] + [kiT] + [qiT[:, k, :] for k in range(4)] + [qT[:, k, :] for k in range(KD)]
            for n, d in enumerate(dst):
                act_e.wait_ge(turn_ps, n + 1)
                copy(d, bank(n % 8)[:, 0:d.shape[1]]).then_inc(turn_ok, 1)
            for n in range(8):
                act_e.wait_ge(idx_ps, n + 1)
                if n >= 2:
                    act_e.wait_ge(relu_used, n - 1)
                keys = P if n < 4 else SEQ
                act_f(split(relu_b[:, n % 2, 0:2 * keys], 2), PS[:, 2 * (n % 3):2 * (n % 3) + 2, 0:keys], ACT.Relu, scale=HD ** -0.5).then_inc(relu_ok, 1)

            def gate_copy(m):
                act_e.wait_ge(gate_ps, m + 1)
                copy(gatesT[:, m, :], bank(6 + m % 2)[:, 0:SEQ]).then_inc(gate_ok, 1)

            for m in range(3):
                gate_copy(m)
            for h in range(HEADS):
                act_e.wait_ge(s_ok, h + 1)
                if h >= 2:
                    act_e.wait_ge(pT_ps, h - 1)
                st = head_stat[:, h % 4]
                act_f(prob[:, h % 2, 0:144], sbuf_s[:, h % 2, 0:144], ACT.Exp, scale=HD ** -0.5, bias=st[:, 2:3], accum_out=st[:, 4:5])
                act_f(prob[:, h % 2, 144:416], sbuf_s[:, h % 2, 144:416], ACT.Exp, scale=HD ** -0.5, bias=st[:, 3:4],
                      accum_out=st[:, 5:6]).then_inc(prob_ok, 1)
                if h + 3 < 16:
                    gate_copy(h + 3)
                act_e.wait_ge(pT_ps, h + 1)
                if h >= 2:
                    act_e.wait_ge(pv_ps, h - 1)
                copy(pT_m[0:N_META, h % 2, :], bank(4)[0:N_META, 0:256]).then_inc(pTm_ok, 1)
                copy(pT_k[:, h % 2, :], bank(2 + h % 2)[:, 0:384]).then_inc(pTk_ok, 1)
            act_e.wait_ge(gate_ok, 16)
            act_f(gatesT[:, 8:16, :], gatesT[:, 8:16, :], ACT.Sigmoid).then_inc(sigm_ok, 1)
            act_f(gatesT[:, 0:8, :], gatesT[:, 0:8, :], ACT.Sigmoid).then_inc(sigm_ok, 1)
            for k in range(KD):
                act_e.wait_ge(aoT_ps, k + 1)
                copy(attnT[:, k, :], bank(k % 4)[:, 0:SEQ]).then_inc(attnT_ok, 1)
            def square(t, c):
                act_e.wait_ge(h2_ok, 2 * t + c + 1)
                act_f(junk[2 * t + c], hrow[:, t, 512 * c:512 * c + 512], ACT.Square, accum_out=rstat[:, 2 * t + c:2 * t + c + 1]).then_inc(sq2, 1)

            def rows_turned(t):
                act_e.wait_ge(hn2T_ps, t + 1)
                copy(hn2T[:, 4:8, P * t:P * t + P], split(bank(5 + 2 * t), 4)).then_inc(h2T_act, 1)

            act_f(stat[:, 10:11], stat[:, 8:9], ACT.Sqrt)
            square(0, 0)
            square(0, 1)
            rows_turned(0)
            square(1, 0)
            square(1, 1)
            rows_turned(1)
            act_e.wait_ge(rstd2, 1)
            act_f(rstat[:, 6:8], rstat[:, 6:8], ACT.Sqrt, scale=1.0 / D, bias=stat[:, 8:9]).then_inc(rstd2, 1)
            act_f(stat[:, 11:12], stat[:, 8:9], ACT.Exp)
            act_e.wait_ge(negv_ok, 1)
            for t in range(RT):
                i = act_f(e4[:, t, 0:4], v8[:, t, 0:4], ACT.Exp, bias=rstat[:, 8 + t:9 + t], accum_out=rstat[:, 10 + t:11 + t])
            i.then_inc(e4_ok, 1)
            act_f(stat[:, 12:13], stat[:, 8:9], ACT.Sigmoid)
            act_e.wait_ge(route_ps, 2)
            copy(dwT[0:EXPERTS].rearrange("p a b -> p (a b)"), bank(7)[0:EXPERTS, 0:256]).then_inc(dwT_ok, 1)

            def tokens_out(u):
                act_e.wait_ge(xrow_ps2, u + 1)
                copy(xrow, bank(6)).then_inc(xrow_sb, 1)

            def unit(u, ahead):
                act_e.wait_ge(selT_ps, u + 1)
                act_e.wait_ge(scat_ps, u + 1)
                copy(selT, bank(7)[:, 0:256]).then_inc(selT_ok, 1)
                act_e.wait_ge(gmin_ok, u + 1)
                act_f(sig, gmin, ACT.Sigmoid, scale=ALPHA).then_inc(sig_ok, 1)
                if ahead:
                    tokens_out(u + 1)
                act_e.wait_ge(actT_ps, u + 1)
                copy(actT, bank(4)).then_inc(actT_ok, 1)
                act_e.wait_ge(dn_free, u * 4 + 4)
                copy(y_sb, bank(7)).then_inc(ysb_ok, 1)

            tokens_out(0)
            with act_e.Fori(0, LOOPED) as u:
                unit(u, True)
            for u in range(LOOPED, EXPERTS):
                unit(u, u < EXPERTS - 1)
            act_e.wait_ge(route_ok, 1)
            over = act_e.value_load(n_over[0:1, 0:1], min_val=0, max_val=OVERFLOW_MAX)
            with act_e.If(over > 0):
                with act_e.Fori(0, over) as j:
                    tokens_out(j + EXPERTS)
                    unit(j + EXPERTS, False)
                    act_e.wait_ge(scat_ps, j + EXPERTS + 2)
            act_f(stat[:, 13:14], stat[:, 8:9], ACT.Sqrt)
            for t in range(RT):
                act_e.wait_ge(*((scat_ps, EXPERTS + 1) if t else (scat_top_ps, EXPERTS)))
                act_f(junk2[t], PS[:, 2 * t:2 * t + 2, :], ACT.Square, accum_out=rstat[:, t:t + 1]).then_inc(sq3, 1)
                act_e.wait_ge(sq3, t + 1)
                act_f(rstat[:, 2 + t:3 + t], rstat[:, t:t + 1], ACT.Sqrt, scale=1.0 / D, bias=stat[:, 8:9]).then_inc(root3, 1)

        @block.vector
        def _(dve):
            V = nc.vector
            chain = [0]

            def link(ins):
                chain[0] += 1
                ins.then_inc(dve_chain, 1)
                dve.wait_ge(dve_chain, chain[0])

            V.memset(small_t[:, 208:312], 0.0).then_inc(zeroed, 1)
            V.memset(stat[:, 8:9], EPS).then_inc(zeroed, 1)
            for i, t in enumerate(NORM_ORDER):
                n = P if t < RT else N_META
                src = hrow[:, t, :] if t < RT else hmeta[0:n, :]
                dve.wait_ge(rstd1, i + 1)
                link(V.reciprocal(stat[0:n, 3 + t:4 + t], stat[0:n, 3 + t:4 + t]))
                V.tensor_scalar(xn[0:n, t, :], src, stat[0:n, 3 + t:4 + t], None, ALU.mult).then_inc(xn_ok, 1)
            dve.wait_ge(cols_ps, 1)
            V.tensor_copy(cols1[:, :], bank(0)[:, 0:P])
            V.tensor_copy(cols2[:, :], bank(0)[:, P:P + 24]).then_inc(cols_ok, 1)
            dve.wait_ge(cols_ok, 1)
            for i, k in enumerate(K_ORDER):
                dve.wait_ge(xnT_ps, i + 1)
                V.tensor_scalar(hnT[:, k, :], bank(k)[:, 0:T_ALL], g1_col[k], None, ALU.mult).then_inc(hnT_ok, 1)
            dve.wait_ge(small_ok, 1)
            dve.wait_ge(vec_in, 48)
            link(V.tensor_tensor(dt_x, small[:, :, 72:104], bc[:, 0, :].unsqueeze(1).broadcast_to([P, 3, 32]), ALU.add))
            V.scalar_tensor_tensor(out=dt_n, in0=dt_x, scalar=-1.0, in1=dt_x, op0=ALU.mult, op1=ALU.min).then_inc(dt_dve, 1)

            def conv(j):
                dve.wait_ge(conv_ps, j + 1)
                if j >= 3:
                    dve.wait_ge(xbc_ok, j - 2)
                ps, ca = bank(1 + j % 7), conv_acc[:, j % 3, :]
                link(V.tensor_scalar(ca, ps[:, 0:T_ALL], conv_col[3][j], None, ALU.mult))
                for back in range(1, CONV_W):
                    i = V.scalar_tensor_tensor(out=ca[:, back:], in0=ps[:, 0:T_ALL - back], scalar=conv_col[3 - back][j],
                                               in1=ca[:, back:], op0=ALU.mult, op1=ALU.add)
                    if back < CONV_W - 1:
                        link(i)
                i.then_inc(conv_ok, 1)

            for j in range(CONV_TILES):
                conv(j)
                if j == 1:
                    dve.wait_ge(dt_act, 1)
                    V.scalar_tensor_tensor(out=dtv, in0=dt_x, scalar=0.0, in1=dt_l, op0=ALU.max, op1=ALU.add).then_inc(dt_dve, 1)
                    dve.wait_ge(dt_dve, 2)
                    V.scalar_tensor_tensor(out=adt, in0=dtv, scalar=-1.0, in1=ea_log.unsqueeze(1).broadcast_to([P, 3, 32]),
                                           op0=ALU.mult, op1=ALU.mult).then_inc(dt_dve, 1)
                if j == 14:
                    dve.wait_ge(dt_act, 2)
                    V.tensor_tensor(wdec, acs[:, 3:6, :], acs[:, 0:3, :], ALU.subtract).then_inc(dt_dve, 1)
            dve.wait_ge(dt_act, 3)
            V.tensor_tensor(wdec, wdec, dtv, ALU.mult).then_inc(dt_dve, 1)

            def per_head(v):
                return v.unsqueeze(2).broadcast_to([P, GH, HD])

            def heads(v):
                return v.rearrange("p (h e) -> p h e", h=GH)

            def decay_args(g, t):
                for hf in range(2):
                    n = 4 * g + 2 * t + hf
                    dve.wait_ge(abc_ps, n + 1)
                    if n >= 2:
                        dve.wait_ge(yd_ps, 2 * g + t)
                    for q in range(4):
                        h = GH * g + 4 * hf + q
                        i = V.tensor_scalar(argm[:, hf, P * q:P * q + P], bank(4 + hf)[:, P * q:P * q + P], acs[:, t, h:h + 1], 0.0,
                                            ALU.subtract, ALU.min)
                    i.then_inc(arg_ok, 1)

            def decay_times_cb(g, t):
                for hf in range(2):
                    dve.wait_ge(exp_ok, 4 * g + 2 * t + hf + 1)
                    V.tensor_tensor(split(argm[:, hf, :], 4), split(argm[:, hf, :], 4),
                                    cbm[:, t, :].unsqueeze(1).broadcast_to([P, 4, P]), ALU.mult).then_inc(decay_ok, 1)

            def y_sum(g, t):
                hs = slice(GH * g, GH * g + GH)
                dve.wait_ge(tanh_ok, 2 * g + t + 1)
                V.scalar_tensor_tensor(out=gated, in0=tanh_z, scalar=1.0, in1=bank(7), op0=ALU.add, op1=ALU.mult).then_inc(z_used, 1)
                dve.wait_ge(yo_ps, 2 * g + t + 1)
                if g:
                    dve.wait_ge(yT_ps, 2 * g)
                link(V.tensor_tensor(heads(yrow[:, t, :]), heads(bank(t)), per_head(eacs[:, t, hs]), ALU.mult))
                dve.wait_ge(yd_ps, 2 * g + t + 1)
                i = V.tensor_tensor(yrow[:, t, :], yrow[:, t, :], bank(6), ALU.add)
                i.then_inc(y_read, 1)
                dve.wait_ge(y_read, 2 * g + t + 1)
                dve.wait_ge(pool_x, 6 * g + (2 if t == 0 else 5))
                link(V.tensor_tensor(yrow[:, t, :], yrow[:, t, :], xsk[:, t, :], ALU.add))
                dve.wait_ge(z_used, 2 * g + t + 1)
                V.scalar_tensor_tensor(out=yrow[:, t, :], in0=yrow[:, t, :], scalar=0.5, in1=gated, op0=ALU.mult, op1=ALU.mult)\
                 .then_inc(y_ok, 1)

            def y_norm(g):
                for t in range(RT):
                    dve.wait_ge(ysq_ok, 2 * g + t + 1)
                    r = ss_y[:, 8 + 2 * g + t:9 + 2 * g + t]
                    link(V.reciprocal(r, r))
                    V.tensor_scalar(yrow[:, t, :], yrow[:, t, :], r, None, ALU.mult).then_inc(yn_ok, 1)

            def y_store(g):
                for t in range(RT):
                    dve.wait_ge(yT_ps, 2 * g + t + 1)
                    V.tensor_tensor(ssmT[:, 4 * g:4 * g + 4, P * t:P * t + P], split(bank(t), 4),
                                    ssmg_cols[:, 4 * g:4 * g + 4].unsqueeze(2).broadcast_to([P, 4, P]), ALU.mult).then_inc(ssmT_ok, 1)

            for g in range(GROUPS):
                hs = slice(GH * g, GH * g + GH)
                decay_args(g, 0)
                dve.wait_ge(brow_ok, g + 1)
                V.tensor_tensor(cbm, split(bank(3)[:, 256:512], 2), tri_le.unsqueeze(1).broadcast_to([P, 2, P]), ALU.mult)\
                 .then_inc(cbm_ok, 1)
                dve.wait_ge(cbm_ok, g + 1)
                decay_times_cb(g, 0)
                if g:
                    y_store(g - 1)
                decay_args(g, 1)
                y_sum(g, 0)
                dve.wait_ge(state_ok, 2 * g + 1)
                link(V.tensor_tensor(heads(prev[:, 1, :]), heads(prev[:, 0, :]), per_head(cdec[:, hs]), ALU.mult))
                dve.wait_ge(state_ps, 2 * g + 2)
                V.tensor_tensor(prev[:, 1, :], prev[:, 1, :], bank(2), ALU.add).then_inc(state_ok, 1)
                decay_times_cb(g, 1)
                y_sum(g, 1)
                y_norm(g)
            y_store(GROUPS - 1)

            def rope(v, tiles, n_heads, tab):
                p = v.shape[0]
                v4 = v.rearrange("p t (h e) -> p t h e", h=n_heads)
                a, b = v4[:, :, :, 0:HALF], v4[:, :, :, HALF:ROT]
                cos, sin = (tab[:, :, c:c + HALF].unsqueeze(2).broadcast_to([p, tiles, n_heads, HALF]) for c in (0, HALF))
                tmp = [rope_tmp[0:p, i, 0:tiles * n_heads * HALF].rearrange("p (t h e) -> p t h e", t=tiles, h=n_heads) for i in range(4)]
                V.tensor_tensor(tmp[0], a, cos, ALU.mult)
                V.tensor_tensor(tmp[1], b, sin, ALU.mult)
                V.tensor_tensor(tmp[2], b, cos, ALU.mult)
                link(V.tensor_tensor(tmp[3], a, sin, ALU.mult))
                V.tensor_tensor(a, tmp[0], tmp[1], ALU.subtract)
                V.tensor_tensor(b, tmp[2], tmp[3], ALU.add).then_inc(rope_ok, 1)
                dve.wait_ge(rope_ok, ropes[0] + 1)
                ropes[0] += 1

            ropes = [0]
            dve.wait_ge(proj_ok, 4)
            rope(kraw[:, 0:2, :], 2, HEADS, rope_tab[:, 0:2, :])
            dve.wait_ge(kmeta_ok, 1)
            rope(kraw[0:N_META, 2:3, :], 1, HEADS, rope_tab[0:N_META, 2:3, :])
            rope(small[:, 0:2, 0:64], 2, 1, rope_tab[:, 0:2, :])
            V.tensor_copy(kidup[:, :, 0:64], small[:, 0:2, 0:64])
            V.tensor_copy(kidup[:, :, 64:128], small[:, 0:2, 0:64])
            V.tensor_scalar(small[:, 0:2, 64:72], small[:, 0:2, 64:72], IDX_HEADS ** -0.5, None, ALU.mult)
            dve.wait_ge(proj_ok, 12)
            rope(qraw, 2, HEADS, rope_tab[:, 0:2, :])
            dve.wait_ge(proj_ok, 14)
            rope(qiraw, 2, IDX_HEADS, rope_tab[:, 0:2, :])

            n = 0
            for t in range(RT):
                keys = P * (t + 1)
                for i in range(4):
                    dve.wait_ge(relu_ok, n + 1)
                    for o in range(2):
                        w = small[:, t, 64 + 2 * i + o:65 + 2 * i + o]
                        r = relu_b[:, n % 2, keys * o:keys * o + keys]
                        if i == 0 and o == 0:
                            link(V.tensor_scalar(score[:, t, 0:keys], r, w, None, ALU.mult))
                        else:
                            j = V.scalar_tensor_tensor(out=score[:, t, 0:keys], in0=r, scalar=w, in1=score[:, t, 0:keys],
                                                       op0=ALU.mult, op1=ALU.add)
                            if o:
                                j.then_inc(relu_used, 1)
                                dve.wait_ge(relu_used, n + 1)
                            else:
                                link(j)
                    n += 1
            for t in range(RT):
                keys = P * (t + 1)
                if t:
                    V.tensor_copy(work[:, t, 0:P], score[:, t, 0:P])
                link(V.tensor_tensor(work[:, t, keys - P:keys], score[:, t, keys - P:keys], cst("causal_neg"), ALU.add))
            for r in range(TOPK_KEYS // 8):
                for t in range(RT):
                    keys = P * (t + 1)
                    j = V.max(top8[:, 64 * t + 8 * r:64 * t + 8 * r + 8], work[:, t, 0:keys])
                link(j)
                for t in range(RT):
                    keys = P * (t + 1)
                    j = V.match_replace(work[:, t, 0:keys], top8[:, 64 * t + 8 * r:64 * t + 8 * r + 8], work[:, t, 0:keys], PICKED)
                link(j)
            V.memset(amask[:, 0:N_META], 0.0)
            V.memset(amask[:, 144:160], 0.0)
            am = [amask[:, 16:144], amask[:, 160:416]]
            for t in range(RT):
                keys = P * (t + 1)
                j = V.tensor_scalar(am[t], work[:, t, 0:keys], PICKED, None, ALU.is_equal)
            link(j)
            for t in range(RT):
                j = V.tensor_tensor(am[t][:, P * t:P * t + P], am[t][:, P * t:P * t + P], cst("causal"), ALU.mult)
            link(j)
            for t in range(RT):
                j = V.tensor_scalar(am[t], am[t], 1.0, 1.0e30, ALU.subtract, ALU.mult)
            j.then_inc(mask_ok, 1)
            dve.wait_ge(mask_ok, 1)

            def head_scores(h):
                dve.wait_ge(s_ps, h + 1)
                if h >= 2:
                    dve.wait_ge(prob_ok, h - 1)
                st, s = head_stat[:, h % 4], sbuf_s[:, h % 2, :]
                link(V.tensor_tensor(s, bank(h % 2)[:, 0:416], amask, ALU.add))
                V.tensor_reduce(st[:, 0:1], s[:, 0:144], AX.X, ALU.max)
                link(V.tensor_reduce(st[:, 1:2], s[:, 144:416], AX.X, ALU.max))
                V.tensor_scalar(st[:, 2:4], st[:, 0:2], -(HD ** -0.5), None, ALU.mult).then_inc(s_ok, 1)

            def head_out(h):
                dve.wait_ge(prob_ok, h + 1)
                st = head_stat[:, h % 4]
                link(V.reciprocal(st[:, 6:8], st[:, 4:6]))
                dve.wait_ge(pv_ps, h + 1)
                for t in range(RT):
                    j = V.tensor_scalar(ao[:, t, HD * h:HD * h + HD], bank(5)[:, P * (h % 2) + HD * t:P * (h % 2) + HD * t + HD],
                                        st[:, 6 + t:7 + t], None, ALU.mult)
                j.then_inc(ao_ok, 1)

            head_scores(0)
            for h in range(HEADS):
                if h + 1 < HEADS:
                    head_scores(h + 1)
                if h:
                    head_out(h - 1)
            head_out(HEADS - 1)
            dve.wait_ge(sigm_ok, 1)
            for m in range(8):
                dve.wait_ge(os_ps, m + 1)
                V.tensor_tensor(gatesT[:, 8 + m, :], bank(6 + m % 2)[:, 0:SEQ], gatesT[:, 8 + m, :], ALU.mult).then_inc(os_ok, 1)
            dve.wait_ge(sigm_ok, 2)
            dve.wait_ge(os_ok, 8)
            for m in range(8):
                dve.wait_ge(oa_ps, m + 1)
                link(V.tensor_tensor(gatesT[:, m, :], bank(4 + m % 2)[:, 0:SEQ], gatesT[:, m, :], ALU.mult))
                V.tensor_tensor(gatesT[:, m, :], gatesT[:, m, :], gatesT[:, 8 + m, :], ALU.add).then_inc(uT_ok, 1)
            def residual(t, c):
                dve.wait_ge(wo_ps, 2 * t + c + 1)
                V.tensor_tensor(hrow[:, t, 512 * c:512 * c + 512], bank(2 * t + c), hrow[:, t, 512 * c:512 * c + 512], ALU.add)\
                 .then_inc(h2_ok, 1)

            def rows_turned(t):
                dve.wait_ge(hn2T_ps, t + 1)
                V.tensor_copy(hn2T[:, 0:4, P * t:P * t + P], split(bank(4 + 2 * t), 4)).then_inc(h2T_dve, 1)

            dve.wait_ge(late_in, 64)
            V.tensor_tensor(w_r, w_r, g2_cols.unsqueeze(2).broadcast_to([P, KD, EXPERTS]), ALU.mult).then_inc(wr_ok, 1)
            residual(0, 0)
            residual(0, 1)
            residual(1, 0)
            rows_turned(0)
            residual(1, 1)
            rows_turned(1)
            dve.wait_ge(sq2, 4)
            V.tensor_tensor(rstat[:, 6:8], rstat[:, 0:4:2], rstat[:, 1:4:2], ALU.add).then_inc(rstd2, 1)
            dve.wait_ge(rstd2, 2)
            link(V.reciprocal(rstat[:, 6:8], rstat[:, 6:8]))
            dve.wait_ge(logit_ps, 2)
            for t in range(RT):
                j = V.scalar_tensor_tensor(out=logit[:, t, :], in0=bank(4 + 2 * t)[:, 0:EXPERTS], scalar=rstat[:, 6 + t:7 + t],
                                           in1=br_bc, op0=ALU.mult, op1=ALU.add)
            link(j)
            for t in range(RT):
                j = V.max(v8[:, t, :], logit[:, t, :])
            link(j)
            V.tensor_scalar(rstat[:, 8:10], v8[:, :, 0:1].rearrange("p a b -> p (a b)"), -1.0, None, ALU.mult).then_inc(negv_ok, 1)
            for t in range(RT):
                j = V.max_index(idx8[:, t, :], v8[:, t, :], logit[:, t, :])
            link(j)
            link(V.tensor_copy(idxf, idx8))
            pick4 = pick.rearrange("p t (i e) -> p t i e", i=TOP_K)
            link(V.tensor_tensor(pick4, cst("experts").unsqueeze(1).unsqueeze(1).broadcast_to([P, 2, TOP_K, EXPERTS]),
                                 idxf[:, :, 0:TOP_K].unsqueeze(3).broadcast_to([P, 2, TOP_K, EXPERTS]), ALU.is_equal))
            dve.wait_ge(e4_ok, 1)
            link(V.reciprocal(rstat[:, 10:12], rstat[:, 10:12]))
            link(V.tensor_tensor(w4[:, :, 0:4], e4[:, :, 0:4], rstat[:, 10:12].unsqueeze(2).broadcast_to([P, 2, 4]), ALU.mult))
            link(V.tensor_tensor(pick4, pick4, w4[:, :, 0:TOP_K].unsqueeze(3).broadcast_to([P, 2, TOP_K, EXPERTS]), ALU.mult))
            link(V.tensor_reduce(dense_w, pick.rearrange("p t (i e) -> p t e i", i=TOP_K), AX.X, ALU.add))
            V.tensor_scalar(routed, dense_w, 0.0, None, ALU.is_gt).then_inc(dense_ok, 1)
            for t in range(RT):
                V.tensor_scalar(hn2[:, t, :], hrow[:, t, :], rstat[:, 6 + t:7 + t], None, ALU.mult).then_inc(hn2_ok, 1)
            dve.wait_ge(route_ps, 1)
            dve.wait_ge(dense_ok, 1)
            link(V.scalar_tensor_tensor(out=posm, in0=split(bank(6)[:, 0:64], 2), scalar=UNROUTED, in1=routed, op0=ALU.add, op1=ALU.mult))
            link(V.tensor_scalar(posm, posm, UNROUTED, None, ALU.subtract))

            def slot_ids(b):
                return slots[:, 0, :] if b is None else slots[:, bass.ds(b, 1), :].rearrange("p b s -> p (b s)")

            def select(u, e, b):
                for t in range(RT):
                    j = V.tensor_scalar(sel[:, t, :], slot_ids(b)[:, 0:SLOTS], posm[:, t, bass.ds(e, 1)], None, ALU.is_equal)
                j.then_inc(sel_ok, 1)
                V.tensor_scalar(one_expert[0:96, :], cst("row_expert")[0:96, :].broadcast_to([96, SLOTS]),
                                cst("experts")[0:96, bass.ds(e, 1)], None, ALU.is_equal).then_inc(hot_ok, 1)

            def tokens_in(u):
                dve.wait_ge(xe_ps, u + 1)
                V.tensor_tensor(xe_flat.rearrange("p (j a s) -> p j a s", j=4, a=2), bank(5).rearrange("p (j a s) -> p j a s", j=4, a=2),
                                g2_cols.rearrange("p (a j) -> p j a", a=2).unsqueeze(3).broadcast_to([P, 4, 2, SLOTS]),
                                ALU.mult).then_inc(xe_ok, 1)

            def unit(u, e, b, ahead):
                for t in range(RT):
                    j = V.tensor_scalar(selw[:, t, :], slot_ids(b), posm[:, t, bass.ds(e, 1)], dense_w[:, t, bass.ds(e, 1)],
                                        ALU.is_equal, ALU.mult)
                j.then_inc(selw_ok, 1)
                if ahead:
                    dve.wait_ge(bias_ps, u + 1)
                    select(u + 1, e + 1, b)
                dve.wait_ge(gu_free, u * KD + KD)
                V.tensor_scalar(gmin, bank(4), LIMIT, None, ALU.min).then_inc(gmin_ok, 1)
                V.tensor_scalar(upc, bank(5), LIMIT, -LIMIT, ALU.min, ALU.max).then_inc(upc_ok, 1)
                dve.wait_ge(gmin_ok, u + 1)
                dve.wait_ge(upc_ok, u + 1)
                V.scalar_tensor_tensor(out=upc, in0=upc, scalar=1.0, in1=gmin, op0=ALU.add, op1=ALU.mult).then_inc(upg_ok, 1)
                dve.wait_ge(upg_ok, u + 1)
                dve.wait_ge(sig_ok, u + 1)
                V.tensor_tensor(act, upc, sig, ALU.mult).then_inc(act_ok, 1)
                if ahead:
                    tokens_in(u + 1)

            select(0, 0, None)
            dve.wait_ge(route_ps, 2)
            V.tensor_copy(count[0:1, :], bank(4)[0:1, 0:32]).then_inc(count_ok, 1)
            dve.wait_ge(count_ok, 1)
            link(V.tensor_tensor(split(flags[0:1, :], 3), count[0:1, :].unsqueeze(1).broadcast_to([1, 3, EXPERTS]),
                                 split(cst("thresholds")[0:1, :], 3), ALU.is_gt))
            link(V.tensor_reduce(n_over_f[0:1, :], flags[0:1, :], AX.X, ALU.add))
            V.tensor_copy(n_over[0:1, :], n_over_f[0:1, :]).then_inc(route_ok, 1)
            dve.wait_ge(route_ok, 1)
            tokens_in(0)
            with dve.Fori(0, LOOPED) as u:
                unit(u, u, None, True)
            for u in range(LOOPED, EXPERTS):
                unit(u, u, None, u < EXPERTS - 1)
            over = dve.value_load(n_over[0:1, 0:1], min_val=0, max_val=OVERFLOW_MAX)
            with dve.If(over > 0):
                link(V.tensor_tensor_scan(seq[0:1, :], ones[0:1, 0:96], flags[0:1, :], 0.0, ALU.mult, ALU.add))
                link(V.tensor_tensor(seq[0:1, :], seq[0:1, :], flags[0:1, :], ALU.mult))
                link(V.tensor_scalar(seq[0:1, :], seq[0:1, :], 1.0, None, ALU.subtract))
                link(V.tensor_tensor(one_hot[0:1], seq[0:1, :].unsqueeze(1).broadcast_to([1, OVERFLOW_MAX, 96]),
                                     cst("turns")[0:1, :].unsqueeze(2).broadcast_to([1, OVERFLOW_MAX, 96]), ALU.is_equal))
                link(V.tensor_tensor(one_hot[0:1], one_hot[0:1], cst("codes")[0:1, :].unsqueeze(1).broadcast_to([1, OVERFLOW_MAX, 96]), ALU.mult))
                link(V.tensor_reduce(codes_f[0:1, :], one_hot[0:1], AX.X, ALU.add))
                V.tensor_copy(codes[0:1, :], codes_f[0:1, :]).then_inc(codes_ok, 1)
                dve.wait_ge(codes_ok, 1)
                with dve.Fori(0, over) as j:
                    jj = nc.s_assert_within(j, 0, OVERFLOW_MAX - 1)
                    code = dve.value_load(codes[0:1, bass.ds(jj, 1)], min_val=0, max_val=4 * EXPERTS - 1)
                    select(jj + EXPERTS, code % EXPERTS, code // EXPERTS)
                    tokens_in(jj + EXPERTS)
                    unit(jj + EXPERTS, code % EXPERTS, code // EXPERTS, False)
                    dve.wait_ge(scat_ps, jj + EXPERTS + 2)
            for t in range(RT):
                dve.wait_ge(root3, t + 1)
                V.reciprocal(rstat[:, 4 + t:5 + t], rstat[:, 2 + t:3 + t]).then_inc(rstd3, 1)
                dve.wait_ge(rstd3, t + 1)
                V.scalar_tensor_tensor(out=split(final[:, t, :], 2), in0=PS[:, 2 * t:2 * t + 2, :], scalar=rstat[:, 4 + t:5 + t],
                                       in1=split(gf_bc, 2), op0=ALU.mult, op1=ALU.mult).then_inc(out_ok, 1)


_INS = ["x", "meta_tokens", "norm1_g", "w_in", "conv_w", "conv_b", "dt_bias", "a_log", "d_skip", "ssm_norm_g",
        "w_o_attn", "w_o_ssm", "w_out", "norm2_g", "w_router", "b_router", "w_gate_up", "b_gate_up",
        "w_down", "b_down", "final_g"]


def kernel(**inputs):
    import numpy as _np
    import concourse.bacc as _bacc
    from concourse import mybir as _mybir
    from concourse.bass_utils import run_bass_kernel_spmd as _run

    nc = _bacc.Bacc("TRN2", target_bir_lowering=False, num_devices=1)
    arrays, args = {}, []
    for name in _INS:
        a = _np.ascontiguousarray(inputs[name])
        arrays[f"in_{name}_dram"] = a
        args.append(nc.dram_tensor(f"in_{name}_dram", a.shape, _mybir.dt.from_np(a.dtype), kind="ExternalInput").ap())
    args.append(nc.dram_tensor("out_dram", (1, SEQ, D), _mybir.dt.float32, kind="ExternalOutput").ap())
    build(nc, *args)
    r = _run(nc, [arrays], core_ids=[0])
    return r.results[0]["out_dram"]
```
